# Optimizing a Trainium2 kernel written in Bass

```python
import jax, jax.numpy as jnp
from jax import lax
import numpy as np

D_MODEL = 2048
BATCH = 1
SEQ = 256
DEPTH = 1

HEAD_DIM = 128
NSA_HEADS = 8
NSA_KV = 2
NSA_WIDTH = NSA_HEADS * HEAD_DIM
DSA_HEADS = 8
DSA_KV = 2
DSA_WIDTH = DSA_HEADS * HEAD_DIM
CMP_LEN = 32
CMP_STRIDE = 16
CMP_HIDDEN = 256
SEL_BLOCK = 64
SEL_TOPN = 16
WINDOW = 512
IDX_HEADS = 16
IDX_DIM = 64
DSA_TOPK_MAX = 256
PLE_DIM = 256
Q_BLOCK = 128
EPS = 1e-6
NEG = -1e30
FORCE_SCORE = 1e4

IN_SPLITS = (
    NSA_HEADS * HEAD_DIM,
    NSA_KV * HEAD_DIM,
    NSA_KV * HEAD_DIM,
    NSA_KV * HEAD_DIM,
    NSA_KV * HEAD_DIM,
    NSA_KV * HEAD_DIM,
    NSA_KV * HEAD_DIM,
    NSA_HEADS * 3,
    NSA_WIDTH,
    DSA_HEADS * HEAD_DIM,
    DSA_KV * HEAD_DIM,
    DSA_KV * HEAD_DIM,
    IDX_HEADS * IDX_DIM,
    IDX_DIM,
    IDX_HEADS,
    DSA_WIDTH,
    D_MODEL,
    D_MODEL,
)
IN_WIDTH = sum(IN_SPLITS)

kernel_name = "hybrid_nsa_dsa_gated_merge"

def _rms(x, g):
    xf = x.astype(jnp.float32)
    y = xf * lax.rsqrt(jnp.mean(xf * xf, axis=-1, keepdims=True) + EPS)
    return (y * g.astype(jnp.float32)).astype(x.dtype)

def _slopes(n):
    return 2.0 ** (-8.0 * jnp.arange(1, n + 1, dtype=jnp.float32) / n)

def _masked_softmax(s, mask):
    return jax.nn.softmax(jnp.where(mask, s, NEG), axis=-1)

def _compress(kv, pe, w1, w2):
    B, S, G, dh = kv.shape
    n_cmp = (S - CMP_LEN) // CMP_STRIDE + 1
    idx = jnp.arange(n_cmp)[:, None] * CMP_STRIDE + jnp.arange(CMP_LEN)[None, :]
    blk = kv[:, idx] + pe[None, None, :, None, :].astype(kv.dtype)
    blk = jnp.moveaxis(blk, 3, 2).reshape(B, n_cmp, G, CMP_LEN * dh)
    return jax.nn.silu(blk @ w1) @ w2

def _cmp_to_sel(n_cmp, n_sel):
    c0 = np.arange(n_cmp)[:, None] * CMP_STRIDE
    s0 = np.arange(n_sel)[None, :] * SEL_BLOCK
    ov = np.clip(np.minimum(c0 + CMP_LEN, s0 + SEL_BLOCK) - np.maximum(c0, s0), 0, None)
    return jnp.asarray(ov / CMP_LEN, dtype=jnp.float32)

def _nsa_mixer(q, kc, vc, ks, vs, kw, vw, gates):
    B, S, H, dh = q.shape
    G = ks.shape[2]
    Hg = H // G
    scale = dh ** -0.5
    slopes = _slopes(H).reshape(G, Hg)
    t = jnp.arange(S)
    qg = q.reshape(B, S, G, Hg, dh)

    n_cmp = kc.shape[1]
    c_end = jnp.arange(n_cmp) * CMP_STRIDE + CMP_LEN - 1
    c_mid = c_end.astype(jnp.float32) - (CMP_LEN - 1) / 2.0
    vis = c_end[None, :] <= t[:, None]
    s = jnp.einsum('btgjd,bngd->bgjtn', qg, kc).astype(jnp.float32) * scale
    s = s - slopes[:, :, None, None] * (t[:, None].astype(jnp.float32) - c_mid[None, :])
    p_cmp = _masked_softmax(s, vis) * (t >= CMP_LEN - 1)[:, None].astype(jnp.float32)
    o_cmp = jnp.einsum('bgjtn,bngd->btgjd', p_cmp.astype(vc.dtype), vc).reshape(B, S, H, dh)

    n_sel = S // SEL_BLOCK
    top_n = min(SEL_TOPN, n_sel)
    imp = jnp.einsum('bgtn,nm->btgm', p_cmp.sum(2), _cmp_to_sel(n_cmp, n_sel))
    m = jnp.arange(n_sel)[None, :]
    blk_t = (t // SEL_BLOCK)[:, None]
    valid = (m <= blk_t)[:, None, :]
    forced = ((m == 0) | (m == blk_t) | (m == blk_t - 1))[:, None, :]
    imp = jnp.where(valid & forced, FORCE_SCORE, jnp.where(valid, imp, -1.0))
    _, sel = lax.top_k(imp, top_n)

    ks_blk = jnp.moveaxis(ks.reshape(B, n_sel, SEL_BLOCK, G, dh), 3, 1).reshape(B, G, n_sel, SEL_BLOCK * dh)
    vs_blk = jnp.moveaxis(vs.reshape(B, n_sel, SEL_BLOCK, G, dh), 3, 1).reshape(B, G, n_sel, SEL_BLOCK * dh)
    kw_pad = jnp.pad(kw, ((0, 0), (WINDOW, 0), (0, 0), (0, 0)))
    vw_pad = jnp.pad(vw, ((0, 0), (WINDOW, 0), (0, 0), (0, 0)))
    n_keys = top_n * SEL_BLOCK

    def chunk(c):
        t0 = c * Q_BLOCK
        tq = t0 + jnp.arange(Q_BLOCK)
        qc = lax.dynamic_slice_in_dim(qg, t0, Q_BLOCK, axis=1)
        sc = jnp.moveaxis(lax.dynamic_slice_in_dim(sel, t0, Q_BLOCK, axis=1), 2, 1)
        idx = sc.reshape(B, G, Q_BLOCK * top_n, 1)
        kg = jnp.take_along_axis(ks_blk, idx, axis=2).reshape(B, G, Q_BLOCK, n_keys, dh)
        vg = jnp.take_along_axis(vs_blk, idx, axis=2).reshape(B, G, Q_BLOCK, n_keys, dh)
        kpos = (sc[..., None] * SEL_BLOCK + jnp.arange(SEL_BLOCK)).reshape(B, G, Q_BLOCK, n_keys)
        dist = (tq[:, None] - kpos).astype(jnp.float32)
        s1 = jnp.einsum('bqgjd,bgqkd->bgjqk', qc, kg).astype(jnp.float32) * scale
        s1 = s1 - slopes[None, :, :, None, None] * dist[:, :, None]
        p1 = _masked_softmax(s1, (dist >= 0)[:, :, None])
        o_slc = jnp.einsum('bgjqk,bgqkd->bqgjd', p1.astype(vg.dtype), vg)
        kwc = lax.dynamic_slice_in_dim(kw_pad, t0, WINDOW + Q_BLOCK, axis=1)
        vwc = lax.dynamic_slice_in_dim(vw_pad, t0, WINDOW + Q_BLOCK, axis=1)
        kpos_w = t0 - WINDOW + jnp.arange(WINDOW + Q_BLOCK)
        dw = tq[:, None] - kpos_w[None, :]
        mw = (dw >= 0) & (dw < WINDOW) & (kpos_w[None, :] >= 0)
        s2 = jnp.einsum('bqgjd,bkgd->bgjqk', qc, kwc).astype(jnp.float32) * scale
        s2 = s2 - slopes[:, :, None, None] * dw.astype(jnp.float32)
        p2 = _masked_softmax(s2, mw)
        o_win = jnp.einsum('bgjqk,bkgd->bqgjd', p2.astype(vwc.dtype), vwc)
        return o_slc, o_win

    o_slc, o_win = lax.map(chunk, jnp.arange(S // Q_BLOCK))
    o_slc = jnp.moveaxis(o_slc, 0, 1).reshape(B, S, H, dh)
    o_win = jnp.moveaxis(o_win, 0, 1).reshape(B, S, H, dh)
    g = jax.nn.sigmoid(gates)
    o = g[..., 0:1] * o_cmp + g[..., 1:2] * o_slc + g[..., 2:3] * o_win
    return o.reshape(B, S, H * dh)

def _dsa_mixer(q, k, v, qi, ki, wi):
    B, S, H, dh = q.shape
    G = k.shape[2]
    Hg = H // G
    scale = dh ** -0.5
    slopes = _slopes(H).reshape(G, Hg)
    topk = min(DSA_TOPK_MAX, S // 4)
    qg = q.reshape(B, S, G, Hg, dh)
    wi = wi.astype(jnp.float32) * IDX_HEADS ** -0.5
    s_all = jnp.arange(S)

    def chunk(c):
        t0 = c * Q_BLOCK
        tq = t0 + jnp.arange(Q_BLOCK)
        qic = lax.dynamic_slice_in_dim(qi, t0, Q_BLOCK, axis=1)
        wic = lax.dynamic_slice_in_dim(wi, t0, Q_BLOCK, axis=1)
        qc = lax.dynamic_slice_in_dim(qg, t0, Q_BLOCK, axis=1)
        rel = jax.nn.relu(jnp.einsum('bqhd,bsd->bqhs', qic, ki).astype(jnp.float32) * IDX_DIM ** -0.5)
        score = jnp.einsum('bqhs,bqh->bqs', rel, wic)
        score = jnp.where(s_all[None, :] <= tq[:, None], score, NEG)
        _, idx = lax.top_k(score, topk)
        kg = jax.vmap(lambda a, i: a[i])(k, idx)
        vg = jax.vmap(lambda a, i: a[i])(v, idx)
        dist = (tq[None, :, None] - idx).astype(jnp.float32)
        s = jnp.einsum('bqgjd,bqkgd->bgjqk', qc, kg).astype(jnp.float32) * scale
        s = s - slopes[:, :, None, None] * dist[:, None, None]
        pr = _masked_softmax(s, (dist >= 0)[:, None, None])
        return jnp.einsum('bgjqk,bqkgd->bqgjd', pr.astype(vg.dtype), vg)

    o = lax.map(chunk, jnp.arange(S // Q_BLOCK))
    return jnp.moveaxis(o, 0, 1).reshape(B, S, H * dh)

def setup_inputs(seed: int = 0) -> dict:
    key = jax.random.key(seed)
    ks = jax.random.split(key, 24)
    L = DEPTH

    def nrm(k, shape, scale):
        return jax.random.normal(k, shape, jnp.float32) * scale

    def gain(k, shape):
        return 1.0 + 0.01 * jax.random.normal(k, shape, jnp.float32)

    return {
        "x": nrm(ks[0], (BATCH, SEQ, D_MODEL), 1.0),
        "p": nrm(ks[1], (DEPTH, BATCH, SEQ, PLE_DIM), 1.0),
        "norm_g": gain(ks[2], (L, D_MODEL)),
        "w_in": nrm(ks[3], (L, D_MODEL, IN_WIDTH), D_MODEL ** -0.5),
        "nsa_q_g": gain(ks[4], (L, HEAD_DIM)),
        "nsa_kc_g": gain(ks[5], (L, HEAD_DIM)),
        "nsa_ks_g": gain(ks[6], (L, HEAD_DIM)),
        "nsa_kw_g": gain(ks[7], (L, HEAD_DIM)),
        "cmp_pe_k": nrm(ks[8], (L, CMP_LEN, HEAD_DIM), 0.1),
        "cmp_w1_k": nrm(ks[9], (L, CMP_LEN * HEAD_DIM, CMP_HIDDEN), (CMP_LEN * HEAD_DIM) ** -0.5),
        "cmp_w2_k": nrm(ks[10], (L, CMP_HIDDEN, HEAD_DIM), CMP_HIDDEN ** -0.5),
        "cmp_pe_v": nrm(ks[11], (L, CMP_LEN, HEAD_DIM), 0.1),
        "cmp_w1_v": nrm(ks[12], (L, CMP_LEN * HEAD_DIM, CMP_HIDDEN), (CMP_LEN * HEAD_DIM) ** -0.5),
        "cmp_w2_v": nrm(ks[13], (L, CMP_HIDDEN, HEAD_DIM), CMP_HIDDEN ** -0.5),
        "dsa_q_g": gain(ks[14], (L, HEAD_DIM)),
        "dsa_k_g": gain(ks[15], (L, HEAD_DIM)),
        "w_up_nsa": nrm(ks[16], (L, NSA_WIDTH, D_MODEL), NSA_WIDTH ** -0.5),
        "w_up_dsa": nrm(ks[17], (L, DSA_WIDTH, D_MODEL), DSA_WIDTH ** -0.5),
        "w_out": nrm(ks[18], (L, D_MODEL, D_MODEL), D_MODEL ** -0.5),
        "ple_norm_g": gain(ks[19], (L, D_MODEL)),
        "w_ple_gate": nrm(ks[20], (L, D_MODEL, D_MODEL), D_MODEL ** -0.5),
        "w_ple_proj": nrm(ks[21], (L, PLE_DIM, D_MODEL), PLE_DIM ** -0.5),
    }

def reference(x, p, norm_g, w_in, nsa_q_g, nsa_kc_g, nsa_ks_g, nsa_kw_g,
              cmp_pe_k, cmp_w1_k, cmp_w2_k, cmp_pe_v, cmp_w1_v, cmp_w2_v,
              dsa_q_g, dsa_k_g, w_up_nsa, w_up_dsa, w_out,
              ple_norm_g, w_ple_gate, w_ple_proj):
    B, S, _ = x.shape
    split_points = [int(v) for v in np.cumsum(IN_SPLITS)[:-1]]

    def heads(a):
        return a.reshape(B, S, -1, HEAD_DIM)

    for i in range(DEPTH):
        h = _rms(x, norm_g[i])
        proj = h @ w_in[i]
        (nq, nkc, nvc, nks, nvs, nkw, nvw, ng, nz,
         dq, dk, dv, iq, ik, iw, dz, mg_nsa, mg_dsa) = jnp.split(proj, split_points, axis=-1)

        q_n = _rms(heads(nq), nsa_q_g[i])
        kc = _rms(_compress(heads(nkc), cmp_pe_k[i], cmp_w1_k[i], cmp_w2_k[i]), nsa_kc_g[i])
        vc = _compress(heads(nvc), cmp_pe_v[i], cmp_w1_v[i], cmp_w2_v[i])
        o_nsa = _nsa_mixer(q_n, kc, vc,
                           _rms(heads(nks), nsa_ks_g[i]), heads(nvs),
                           _rms(heads(nkw), nsa_kw_g[i]), heads(nvw),
                           ng.reshape(B, S, NSA_HEADS, 3))
        o_nsa = o_nsa * jax.nn.silu(nz)

        o_dsa = _dsa_mixer(_rms(heads(dq), dsa_q_g[i]), _rms(heads(dk), dsa_k_g[i]), heads(dv),
                           iq.reshape(B, S, IDX_HEADS, IDX_DIM), ik, iw)
        o_dsa = o_dsa * jax.nn.silu(dz)

        y = jax.nn.sigmoid(mg_nsa) * (o_nsa @ w_up_nsa[i]) + jax.nn.sigmoid(mg_dsa) * (o_dsa @ w_up_dsa[i])
        x = x + y @ w_out[i]

        x = x + (p[i] @ w_ple_proj[i]) * jax.nn.sigmoid(_rms(x, ple_norm_g[i]) @ w_ple_gate[i])
    return x


_drawn_inputs = setup_inputs


def setup_inputs(seed=0):
    import zlib

    import numpy as np

    out = dict(_drawn_inputs(seed))
    spreads = {}
    factors = {'norm_g': 3.732,
     'nsa_q_g': 8.0,
     'nsa_kc_g': 36.139,
     'nsa_ks_g': 8.0,
     'nsa_kw_g': 8.0,
     'cmp_pe_k': 8.0,
     'cmp_w1_k': 2.778,
     'cmp_w2_k': 2.702,
     'cmp_pe_v': 6.647,
     'dsa_q_g': 8.0,
     'dsa_k_g': 8.0,
     'ple_norm_g': 64.0}
    for name, (base, spread) in spreads.items():
        noise = np.random.default_rng([zlib.crc32(name.encode()), seed]).standard_normal(out[name].shape)
        drawn = base * np.exp(spread * noise) if base else spread * noise
        out[name] = __import__('jax').numpy.asarray(drawn.astype(out[name].dtype))
    for name, factor in factors.items():
        out[name] = (out[name] * factor).astype(out[name].dtype)
    return out
```

```python
from contextlib import ExitStack

import concourse.bass as bass
from concourse import mybir

F32 = mybir.dt.float32
F32R = mybir.dt.float32r
ALU = mybir.AluOpType
ACT = mybir.ActivationFunctionType

P = 128
D = 2048
T = 256
TT = T // P
KD = D // P
HEADS = 8
DH = 128
GROUPS = 2
HID = 256
CLEN, CSTR = 32, 16
NC = (T - CLEN) // CSTR + 1
NB = GROUPS * NC
IH, ID = 16, 64
TOPK = T // 4
NCOL = 512
EPS = 1e-6
FILL = -1e34
NEG = -1e30
TAKEN = -3e38

C_NQ, C_KC, C_KS, C_KW, C_NG, C_NZ = 0, 1024, 1536, 2048, 2560, 2584
C_DQ, C_DK, C_IQ, C_IK, C_DZ, C_MG = 3608, 4632, 5144, 6168, 6248, 7272
N_SMALL = 24 + 80

TH_KC, TH_KS, TH_KW, TH_DK, TH_NG, TH_IK, TH_IW, TH_IK2 = 1024, 1536, 2048, 2560, 3072, 3096, 3160, 3200

P_A1, P_A0, P_A2, P_A3, P_A4, P_W1K, P_W1V, P_A5, P_A6, P_Q0 = 0, 8, 10, 18, 26, 34, 42, 50, 58, 66
P_L = 74
P_L7 = P_L + 16 * (HEADS - 1)
P_U = P_L7 + 8
P_PP = P_U + 32
P_O = P_PP + 4
P_G = P_O + 32
N_PIECES = P_G + 32
AHEAD = 2
RAW, RING = 4, 4

V_NORM, V_PLE, V_NQ, V_KC, V_KS, V_KW, V_DQ, V_DK, V_PEK, V_PEV = 0, 16, 32, 33, 34, 35, 36, 37, 38, 70
N_VEC = 102

BT, BS0, BS1, BO = 0, 1, 2, 3
T_VEC, T_PLE, T_IK, T_IQ, T_KC, T_VC, T_KS, T_HID, T_KC2, T_KCN, T_KW, T_DK = 1, 4, 5, 6, 10, 11, 12, 13, 14, 15, 16, 17
T_L, T_Y, T_X = 18, 58, 62
S_IDX, S_L = 3, 11
O_L, O_Y, O_X = 3, 19, 23


def build(nc, x, p, norm_g, w_in, nsa_q_g, nsa_kc_g, nsa_ks_g, nsa_kw_g, cmp_pe_k, cmp_w1_k, cmp_w2_k,
          cmp_pe_v, cmp_w1_v, cmp_w2_v, dsa_q_g, dsa_k_g, w_up_nsa, w_up_dsa, w_out, ple_norm_g,
          w_ple_gate, w_ple_proj, out):
    ctx = ExitStack()

    def sb(name, shape, dt=F32, stack=None):
        return (stack or ctx).enter_context(nc.sbuf_tensor(name, shape, dt))

    def sem(name):
        return ctx.enter_context(nc.semaphore(name))

    with ctx:
        raw = sb("raw", [P, RAW, 2, 1024])
        w_hi = sb("w_hi", [P, RING, 1024], F32R)
        w_lo = sb("w_lo", [P, RING, 1024], F32R)
        hT_hi = sb("hT_hi", [P, KD, T], F32R)
        hT_lo = sb("hT_lo", [P, KD, T], F32R)
        th = sb("th", [P, TT, 2 * D])
        kT = sb("kT", [P, 3, GROUPS, T])
        v_all = sb("v_all", [P, 3, TT, GROUPS, DH])
        kcT = sb("kcT", [P, NB])
        vc = sb("vc", [NC, GROUPS, DH])
        dist = sb("dist", [P, 3 * P])
        dist_dsa = sb("dist_dsa", [P, 3 * P])
        dist_c = sb("dist_c", [P, TT, NC])
        ident = sb("ident", [P, P])
        vecT = sb("vecT", [P, N_VEC])
        k_gain = sb("k_gain", [P, 4])
        slopes = sb("slopes", [P, HEADS])
        inv_slopes = sb("inv_slopes", [P, HEADS, 4])
        slope = sb("slope", [P, 1])
        fence_col = sb("fence_col", [P, 3])
        m_half = sb("m_half", [P, 16])
        q_eps = sb("q_eps", [P, 4])
        row_mask = sb("row_mask", [P, TT])
        gates = sb("gates", [P, TT, HEADS, 4])
        pT_hi = sb("pT_hi", [P, 2, T], F32R)
        pT_lo = sb("pT_lo", [P, 2, T], F32R)
        ssx = sb("ssx", [P, TT])
        rstd = sb("rstd", [P, TT])
        half_rstd_x = sb("half_rstd_x", [P, TT])
        ssk = sb("ssk", [P, 3, 4])
        rk = sb("rk", [P, 3, 4])
        ssc = sb("ssc", [NB, 1])
        rc = sb("rc", [NB, 1])
        ssq = sb("ssq", [P, 4])
        rq = sb("rq", [P, 4])
        mx = sb("mx", [P, 8])
        neg_mx = sb("neg_mx", [P, 8])
        rowsum = sb("rowsum", [P, TT, 4])
        rrow = sb("rrow", [P, TT, 4])
        coef = sb("coef", [P, TT, 4])
        ssp = sb("ssp", [P, TT, 4])
        ssp2 = sb("ssp2", [P, TT])
        half_rstd = sb("half_rstd", [P, TT])

        with ExitStack() as st:
            x_nat = sb("x_nat", [P, TT, D], stack=st)
        with ExitStack() as st:
            kvT = sb("kvT", [P, 2, GROUPS, T], stack=st)
            xf = sb("xf", [P, 2, CLEN, NB], stack=st)
            x_hi = sb("x_hi", [P, 2 * CLEN * NB + P - NB], F32R, stack=st)
            x_lo = sb("x_lo", [P, 2 * CLEN * NB + P - NB], F32R, stack=st)
        oT_hi = sb("oT_hi", [P, 2 * HEADS, T], F32R)
        oT_lo = sb("oT_lo", [P, 2 * HEADS, T], F32R)

        with ExitStack() as st:
            iqT = sb("iqT", [P, IH // 2, T], stack=st)
            ikT = sb("ikT", [P, T], stack=st)
            rel = sb("rel", [P, 2, 3 * P], stack=st)
            score = sb("score", [P, 3 * P], stack=st)
            work = sb("work", [P, 3 * P], stack=st)
            top8 = sb("top8", [P, TT, 8], stack=st)
            tmp24 = sb("tmp24", [P, TT, 24], stack=st)
            p_nat = sb("p_nat", [P, TT, 256], stack=st)
            vecs = sb("vecs", [N_VEC, P], stack=st)
            hz = sb("hz", [NB, 2, HID], stack=st)
            hth = sb("hth", [NB, 2, HID], stack=st)
            hidT = sb("hidT", [P, 4, NB], stack=st)
            kc_nat = sb("kc_nat", [NB, DH], stack=st)
            kc_junk = sb("kc_junk", [NB, DH], stack=st)
            w2 = sb("w2", [P, 2, 2, DH], stack=st)
        with ExitStack() as st:
            q_raw = sb("q_raw", [P, TT, 2, 2, P], stack=st)
            z_gate = sb("z_gate", [P, TT, 2, P], stack=st)
            q_n = sb("q_n", [P, TT, 2, P], stack=st)
            qT = sb("qT", [P, 2, T], stack=st)
            prob = sb("prob", [P, 3, 3 * P], stack=st)
            prob_c = sb("prob_c", [P, TT, NC], stack=st)
            probT = sb("probT", [P, 3, 3 * P], stack=st)
            prob_cT = sb("prob_cT", [NC, T], stack=st)
            o_nat = sb("o_nat", [P, 2, TT, P], stack=st)
        xr = sb("xr", [P, TT, D])
        stage = sb("stage", [P, TT, NCOL])

        acc = [[ctx.enter_context(nc.psum_tensor(f"acc{b}{t}", [P, NCOL], F32)) for t in range(TT)] for b in range(2)]
        aux = [ctx.enter_context(nc.psum_tensor(n, [P, 512], F32)) for n in ("aux_t", "aux_s0", "aux_s1", "aux_o")]

        x_first_in, x_in, vec_in, p_in, w2_in, xr_in, stored = (sem(n) for n in ("x_first_in", "x_in", "vec_in", "p_in", "w2_in", "xr_in", "stored"))
        landed = [sem(f"landed{s}") for s in range(RAW)]
        hi_ready, lo_ready, piece_used = sem("hi_ready"), sem("lo_ready"), sem("piece_used")
        acc_out = [sem(f"acc_out{b}") for b in range(2)]
        filled = [sem(f"filled_{n}") for n in ("t", "s0", "s1", "o")]
        drained = [sem(f"drained_{n}") for n in ("t", "s0", "s1", "o")]
        consts, masks, ss_x, rstd_ready, xn_ready = (sem(n) for n in ("consts", "masks", "ss_x", "rstd_ready", "xn_ready"))
        gain_ready, t_hi = sem("gain_ready"), sem("t_hi")
        p_hi, p_ready, ng_tanh, gates_ready, gates_step = (sem(n) for n in ("p_hi", "p_ready", "ng_tanh", "gates_ready", "gates_step"))
        rel_ready, scored, masked, topk_step, dsa_ready = (sem(n) for n in ("rel_ready", "scored", "masked", "topk_step", "dsa_ready"))
        ss_k, rk_step, rk_ready, kn_ready = (sem(n) for n in ("ss_k", "rk_step", "rk_ready", "kn_ready"))
        xf_ready, x_hi_ready, x_lo_ready, x_pad = (sem(n) for n in ("xf_ready", "x_hi_ready", "x_lo_ready", "x_pad"))
        hz_ready, hid_tanh, hid_ready, kc_out, ss_c, kcn_ready = (sem(n) for n in ("hz_ready", "hid_tanh", "hid_ready", "kc_out", "ss_c", "kcn_ready"))
        q_out, z_tanh, ss_q, rq_step, rq_ready, qn_ready, z_ready, slope_ready = (
            sem(n) for n in ("q_out", "z_tanh", "ss_q", "rq_step", "rq_ready", "qn_ready", "z_ready", "slope_ready"))
        neg_ready, exp_ready, coef_step, coef_ready, o_step, o_ready, o_hi = (
            sem(n) for n in ("neg_ready", "exp_ready", "coef_step", "coef_ready", "o_step", "o_ready", "o_hi"))
        y_ready, y_hi, ple_made = sem("y_ready"), sem("y_hi"), sem("ple_made")
        x2_ss, ss2_step, r2_ready, x2_hi = (sem(n) for n in ("x2_ss", "ss2_step", "r2_ready", "x2_hi"))
        g_tanh, out_ready = sem("g_tanh"), sem("out_ready")

        n_dmas = {P_A0 // 2: 4}
        for c in range(P_Q0 // 2, P_L // 2):
            n_dmas[c] = 4
        for h in range(HEADS - 1):
            for c in range(P_L // 2 + 8 * h + 4, P_L // 2 + 8 * h + 8):
                n_dmas[c] = 4
        landed_at, count = [], [0] * RAW
        for c in range(N_PIECES // 2):
            count[c % RAW] += 16 * n_dmas.get(c, 1)
            landed_at.append(count[c % RAW])

        def wait_landed(eng, c, i=0, per=0):
            step = landed_at[c + per] - landed_at[c] if per else 0
            eng.wait_ge(landed[c % RAW], i * step + landed_at[c])

        block = ctx.enter_context(nc.Block())

        @block.sync
        def _(sp):
            def load_x(c0, c1):
                sp.dma_start(x_nat[:, :, c0:c1], x[0, :, c0:c1].rearrange("(t p) n -> p t n", p=P)
                             ).then_inc(x_in if c0 else x_first_in, 16)

            def slot_free(c, i=0, per=0):
                if c >= RAW:
                    sp.wait_ge(lo_ready, i * 2 * per + 2 * (c - RAW) + 2)

            def load(c, src, i=0, per=0):
                slot_free(c, i, per)
                sp.dma_start(raw[:, c % RAW, :, :].rearrange("p a (k n) -> p (a k) n", n=NCOL),
                             src.rearrange("(k p) n -> p k n", p=P)).then_inc(landed[c % RAW], 16)

            def load_block(c0, w, col, i=0, per=0):
                for q in range(4):
                    load(c0 + q, w[q * 4 * P:(q + 1) * 4 * P, col], i, per)

            def load_qz(c0, h, i=0, per=0):
                for q in range(4):
                    c = c0 + q
                    slot_free(c, i, per)
                    rows = w_in[0, q * 4 * P:(q + 1) * 4 * P, :]
                    dst = raw[:, c % RAW, :, :].rearrange("p a (k s n) -> p (a k) s n", s=4, n=P)
                    for s, col in enumerate((C_NQ, C_NZ, C_DQ, C_DZ)):
                        sp.dma_start(dst[:, :, s, :], rows[:, bass.ds(h * P + col, P)].rearrange("(k p) n -> p k n", p=P)
                                     ).then_inc(landed[c % RAW], 16)

            wi = w_in[0]
            load_x(0, NCOL)
            load(0, wi[0:4 * P, C_IQ:C_IQ + NCOL])
            load_x(NCOL, D)
            for c in range(1, 4):
                load(c, wi[c * 4 * P:(c + 1) * 4 * P, C_IQ:C_IQ + NCOL])
            c = P_A0 // 2
            slot_free(c)
            for half in range(2):
                dst = raw[:, c % RAW, half, 0:8 * N_SMALL].rearrange("p (k n) -> p k n", n=N_SMALL)
                rows = wi[half * 8 * P:(half + 1) * 8 * P, :].rearrange("(k p) n -> p k n", p=P)
                sp.dma_start(dst[:, :, 0:24], rows[:, :, C_NG:C_NG + 24]).then_inc(landed[c % RAW], 16)
                sp.dma_start(dst[:, :, 24:N_SMALL], rows[:, :, C_IK:C_IK + 80]).then_inc(landed[c % RAW], 16)
            load_block(P_A2 // 2, wi, slice(C_IQ + NCOL, C_IQ + 2 * NCOL))
            load_block(P_A3 // 2, wi, slice(C_KC, C_KC + NCOL))
            load_block(P_A4 // 2, wi, slice(C_KS, C_KS + NCOL))
            for c0, w1 in ((P_W1K // 2, cmp_w1_k), (P_W1V // 2, cmp_w1_v)):
                for q in range(4):
                    c = c0 + q
                    slot_free(c)
                    sp.dma_start(raw[:, c % RAW, :, :].rearrange("p a (k n) -> p (a k) n", n=HID),
                                 w1[0, q * 8 * P:(q + 1) * 8 * P, :].rearrange("(k p) n -> p k n", p=P)
                                 ).then_inc(landed[c % RAW], 16)
            load_block(P_A5 // 2, wi, slice(C_KW, C_KW + NCOL))
            load_block(P_A6 // 2, wi, slice(C_DK, C_DK + NCOL))
            load_qz(P_Q0 // 2, 0)
            with sp.Fori(0, HEADS - 1) as i:
                load_block(P_L // 2, wi, bass.ds(i * NCOL + C_MG, NCOL), i, 8)
                load_qz(P_L // 2 + 4, i + 1, i, 8)
            load_block(P_L7 // 2, wi, slice(C_MG + 7 * NCOL, C_MG + 8 * NCOL))
            with sp.Fori(0, 4) as j:
                for q in range(2):
                    for b, w in enumerate((w_up_nsa, w_up_dsa)):
                        load(P_U // 2 + 2 * q + b, w[0, q * 4 * P:(q + 1) * 4 * P, bass.ds(j * NCOL, NCOL)], j, 4)
            for q in range(2):
                c = P_PP // 2 + q
                slot_free(c)
                sp.dma_start(raw[:, c % RAW, :, :], w_ple_proj[0, :, q * 2 * NCOL:(q + 1) * 2 * NCOL].rearrange(
                    "(k p) n -> p k n", p=P)).then_inc(landed[c % RAW], 16)
            sp.wait_ge(drained[BT], T_Y - 1)
            for t in range(TT):
                sp.dma_start(xr[:, t, :], x[0, t * P:(t + 1) * P, :]).then_inc(xr_in, 16)
            with sp.Fori(0, 4) as j:
                load_block(P_O // 2, w_out[0], bass.ds(j * NCOL, NCOL), j, 4)
            with sp.Fori(0, 4) as j:
                load_block(P_G // 2, w_ple_gate[0], bass.ds(j * NCOL, NCOL), j, 4)
            for j in range(4):
                for t in range(TT):
                    sp.wait_ge(out_ready, 2 * j + t + 1)
                    sp.dma_start(out[0, t * P:(t + 1) * P, j * NCOL:(j + 1) * NCOL],
                                 xr[:, t, j * NCOL:(j + 1) * NCOL]).then_inc(stored, 16)
            sp.wait_ge(stored, 16 * 8)

        @block.gpsimd
        def _(pool):
            g = nc.gpsimd
            g.memset(ident[:, :], 0.0).then_inc(consts, 1)
            g.memset(m_half[:, :], -0.5).then_inc(consts, 1)
            g.memset(q_eps[:, :], DH * EPS).then_inc(consts, 1)
            pool.wait_ge(consts, 3)
            g.affine_select(out=ident[:, :], in_=ident[:, :], compare_op=ALU.not_equal, fill=1.0, base=0,
                            pattern=[[-1, P]], channel_multiplier=1).then_inc(consts, 1)

            pool.wait_ge(ss_x, 2)
            g.tensor_scalar(rstd[:, :], ssx[:, :], 1.0 / D, EPS, ALU.mult, ALU.add).then_inc(rstd_ready, 1)
            pool.wait_ge(rstd_ready, 1)
            g.tensor_tensor(rstd[:, :], rstd[:, :], m_half[:, 0:TT], ALU.pow).then_inc(rstd_ready, 1)
            pool.wait_ge(rstd_ready, 2)
            g.tensor_scalar(half_rstd_x[:, :], rstd[:, :], 0.5, None, ALU.mult).then_inc(rstd_ready, 1)

            g.iota(dist[:, 0:P], pattern=[[1, P]], base=0, channel_multiplier=-1,
                   allow_small_or_imprecise_dtypes=True).then_inc(masks, 1)
            g.iota(dist[:, P:], pattern=[[1, T]], base=-P, channel_multiplier=-1,
                   allow_small_or_imprecise_dtypes=True).then_inc(masks, 1)
            for t in range(TT):
                g.iota(dist_c[:, t, :], pattern=[[CSTR, NC]], base=-P * t, channel_multiplier=-1,
                       allow_small_or_imprecise_dtypes=True).then_inc(masks, 1)
            g.memset(row_mask[:, :], 1.0).then_inc(masks, 1)
            for h in range(HEADS):
                g.memset(slopes[:, h:h + 1], 2.0 ** -(h + 1)).then_inc(masks, 1)
                g.memset(inv_slopes[:, h, :], 2.0 ** (h + 1)).then_inc(masks, 1)
            g.memset(gates[:, :, :, 3], 0.5).then_inc(masks, 1)
            pool.wait_ge(masks, 6 + 2 * HEADS)
            g.affine_select(out=dist[:, 0:P], in_=dist[:, 0:P], compare_op=ALU.is_ge, fill=FILL, base=0,
                            pattern=[[-1, P]], channel_multiplier=1).then_inc(masks, 1)
            g.affine_select(out=dist[:, P:], in_=dist[:, P:], compare_op=ALU.is_ge, fill=FILL, base=P,
                            pattern=[[-1, T]], channel_multiplier=1).then_inc(masks, 1)
            g.tensor_scalar(dist_c[:, :, :], dist_c[:, :, :], CLEN - 1 - (CLEN - 1) / 2.0, None, ALU.add).then_inc(masks, 1)
            g.affine_select(out=row_mask[:, 0:1], in_=row_mask[:, 0:1], compare_op=ALU.is_ge, fill=0.0,
                            base=-(CLEN - 1), pattern=[[0, 1]], channel_multiplier=1).then_inc(masks, 1)
            pool.wait_ge(masks, 10 + 2 * HEADS)
            for t in range(TT):
                g.affine_select(out=dist_c[:, t, :], in_=dist_c[:, t, :], compare_op=ALU.is_ge, fill=FILL,
                                base=P * t - (CLEN - 1), pattern=[[-CSTR, NC]], channel_multiplier=1).then_inc(masks, 1)

            pool.wait_ge(scored, 2 * IH)
            g.affine_select(out=work[:, 0:P], in_=score[:, 0:P], compare_op=ALU.is_ge, fill=NEG, base=0,
                            pattern=[[-1, P]], channel_multiplier=1).then_inc(masked, 1)
            g.affine_select(out=work[:, P:], in_=score[:, P:], compare_op=ALU.is_ge, fill=NEG, base=P,
                            pattern=[[-1, T]], channel_multiplier=1).then_inc(masked, 1)

            g_view = [[kvT[:, a, b, :].rearrange("p (n l) -> p l n", l=CSTR) for b in range(GROUPS)] for a in range(2)]
            pool.wait_ge(drained[BO], 2)
            for buf in (x_hi, x_lo):
                g.memset(buf[:, 2 * CLEN * NB:].bitcast(F32), 0.0).then_inc(x_pad, 1)
            for kv in range(2):
                pool.wait_ge(drained[BT], T_KC + kv)
                for grp in range(GROUPS):
                    for half in range(CLEN // CSTR):
                        l0 = half * CSTR
                        pe0 = (V_PEK, V_PEV)[kv] + l0
                        g.tensor_tensor(xf[:, kv, l0:l0 + CSTR, grp * NC:(grp + 1) * NC],
                                        g_view[kv][grp][:, :, half:half + NC],
                                        vecT[:, pe0:pe0 + CSTR].unsqueeze(2).to_broadcast([P, CSTR, NC]),
                                        ALU.add).then_inc(xf_ready, 1)

            def k_power(n):
                pool.wait_ge(ss_k, 4 * (n + 1))
                g.tensor_scalar(rk[:, n, :], ssk[:, n, :], 1.0 / DH, EPS, ALU.mult, ALU.add).then_inc(rk_step, 1)
                pool.wait_ge(rk_step, n + 1)
                g.tensor_tensor(rk[:, n, :], rk[:, n, :], m_half[:, 0:4], ALU.pow).then_inc(rk_ready, 1)

            k_power(0)
            pool.wait_ge(ss_c, 1)
            g.tensor_scalar(rc[:, :], ssc[:, :], 1.0 / DH, EPS, ALU.mult, ALU.add).then_inc(ss_c, 1)
            pool.wait_ge(ss_c, 2)
            g.tensor_tensor(rc[:, :], rc[:, :], m_half[0:NB, 0:1], ALU.pow).then_inc(ss_c, 1)
            k_power(1)
            k_power(2)

            def q_power(i):
                pool.wait_ge(ss_q, i * 4 + 4)
                g.tensor_tensor(rq[:, :], ssq[:, :], q_eps[:, :], ALU.add).then_inc(rq_step, 1)
                pool.wait_ge(rq_step, i * 2 + 1)
                g.tensor_tensor(rq[:, :], rq[:, :], m_half[:, 0:4], ALU.pow).then_inc(rq_step, 1)
                pool.wait_ge(rq_step, i * 2 + 2)
                s = inv_slopes[:, bass.ds(i, 1), :].rearrange("p a b -> p (a b)")
                g.tensor_tensor(rq[:, :], rq[:, :], s, ALU.mult).then_inc(rq_ready, 1)

            with pool.Fori(0, HEADS) as i:
                q_power(i)

            pool.wait_ge(x2_ss, 8)
            g.tensor_tensor(ssp[:, :, 0:2], ssp[:, :, 0:2], ssp[:, :, 2:4], ALU.add).then_inc(ss2_step, 1)
            pool.wait_ge(ss2_step, 1)
            g.tensor_tensor(ssp2[:, :], ssp[:, :, 0], ssp[:, :, 1], ALU.add).then_inc(ss2_step, 1)
            pool.wait_ge(ss2_step, 2)
            g.tensor_scalar(ssp2[:, :], ssp2[:, :], 1.0 / D, EPS, ALU.mult, ALU.add).then_inc(ss2_step, 1)
            pool.wait_ge(ss2_step, 3)
            g.tensor_tensor(ssp2[:, :], ssp2[:, :], m_half[:, 0:TT], ALU.pow).then_inc(ss2_step, 1)
            pool.wait_ge(ss2_step, 4)
            g.tensor_scalar(half_rstd[:, :], ssp2[:, :], 0.5, None, ALU.mult).then_inc(r2_ready, 1)

        @block.scalar
        def _(act):
            s = nc.scalar
            row = 0
            for v in (norm_g[0].rearrange("(a b) -> a b", b=P), ple_norm_g[0].rearrange("(a b) -> a b", b=P),
                      nsa_q_g, nsa_kc_g, nsa_ks_g, nsa_kw_g, dsa_q_g, dsa_k_g, cmp_pe_k[0], cmp_pe_v[0]):
                n = v.shape[0]
                act.dma_start(vecs[row:row + n, :], v).then_inc(vec_in, 16)
                row += n
            act.dma_start(p_nat[:, :, :], p[0, 0].rearrange("(t p) n -> p t n", p=P)).then_inc(p_in, 16)
            for kv, w in enumerate((cmp_w2_k, cmp_w2_v)):
                act.dma_start(w2[:, kv, :, :], w[0].rearrange("(k p) n -> p k n", p=P)).then_inc(w2_in, 16)

            def rounded(k0, i=0, per=0):
                wait_landed(act, k0 // 2, i, per // 2)
                if k0 >= RING:
                    act.wait_ge(piece_used, i * per + k0 - RING + 1)
                n = 8 * N_SMALL if P_A0 <= k0 < P_A2 else 1024
                s.activation(w_hi[:, k0 % RING, 0:n], raw[:, (k0 // 2) % RAW, k0 % 2, 0:n], ACT.Copy).then_inc(hi_ready, 1)

            def copied(b, n, dst, src, scale=1.0):
                act.wait_ge(filled[b], n)
                s.activation(dst, src, ACT.Copy, scale=scale).then_inc(drained[b], 1)

            def evacuated(b, end, parts, scale=None):
                if end:
                    act.wait_ge(piece_used, end)
                for t, dst, lo, hi in parts:
                    src = acc[b][t][:, lo:hi]
                    if len(dst.shape) == 3:
                        src = src.rearrange("p (g d) -> p g d", g=GROUPS)
                    e = s.activation(dst, src, ACT.Copy, scale=scale or rstd[:, t:t + 1])
                e.then_inc(acc_out[b], 1)

            def hT_upper(u):
                b, n = (BT, BS0, BS1, BO)[u % 4], (2, 1, 1, 1)[u % 4] + u // 4
                act.wait_ge(filled[b], n)
                if u == 0:
                    act.wait_ge(drained[BT], T_VEC)
                for kt in (2 * u, 2 * u + 1):
                    s.activation(hT_hi[:, kt, :], aux[b][:, (kt % 2) * T:(kt % 2 + 1) * T], ACT.Copy,
                                 scale=vecT[:, V_NORM + kt:V_NORM + kt + 1]).then_inc(t_hi, 1)

            def index_head(hh):
                b = BS0 + hh % 2
                act.wait_ge(filled[b], S_IDX + hh // 2)
                if hh >= 2:
                    act.wait_ge(scored, 2 * (hh - 1))
                s.activation(rel[:, hh % 2, :], aux[b][:, 0:3 * P], ACT.Relu).then_inc(drained[b], 1)

            def hidden(kv):
                act.wait_ge(piece_used, (P_W1V, P_A5)[kv])
                b = 1 - kv
                s.activation(hz[:, kv, :], acc[b][kv][0:NB, 0:HID], ACT.Copy).then_inc(hz_ready, 1)
                s.activation(hth[:, kv, :], acc[b][kv][0:NB, 0:HID], ACT.Tanh, scale=0.5).then_inc(acc_out[b], 1)

            for k in range(AHEAD):
                hT_upper(k)
                rounded(k)
            for k in range(P_L):
                if k + AHEAD < KD // 2:
                    hT_upper(k + AHEAD)
                rounded(k + AHEAD)
                if k == 3:
                    act.wait_ge(x_first_in, 16)
                    act.wait_ge(x_in, 16)
                    s.activation(th[:, 0, D:2 * D], x_nat[:, 0, :], ACT.Square, accum_out=ssx[:, 0:1]).then_inc(ss_x, 1)
                if k == P_A0:
                    act.wait_ge(filled[BT], T_PLE)
                    s.activation(pT_hi[:, :, :], aux[BT][:, :].rearrange("p (k t) -> p k t", k=2), ACT.Copy).then_inc(p_hi, 1)
                if k == P_A2:
                    evacuated(1, P_A2, [(t, th[:, t, TH_NG:TH_NG + N_SMALL], 0, N_SMALL) for t in range(TT)]
                              + [(t, th[:, t, TH_IK2 + d * ID:TH_IK2 + (d + 1) * ID], 24, 24 + ID)
                                 for t in range(TT) for d in range(2)])
                if k == P_A2 + 3:
                    act.wait_ge(acc_out[1], 1)
                    s.activation(tmp24[:, :, :], th[:, :, TH_NG:TH_NG + 24], ACT.Tanh, scale=0.5).then_inc(ng_tanh, 1)
                if k == 12:
                    copied(BT, T_IK, ikT[:, :], aux[BT][:, 0:T])
                if k == P_A0:
                    act.wait_ge(rstd_ready, 3)
                    evacuated(0, P_A0, [(t, th[:, t, 0:NCOL], 0, NCOL) for t in range(TT)])
                for u, at in enumerate((13, 14, 20, 21)):
                    if k == at:
                        copied(BT, T_IQ + u, iqT[:, 2 * u:2 * u + 2, :], aux[BT][:, :].rearrange("p (k t) -> p k t", k=2))
                for hh in range(0, IH, 2):
                    if k == (15 + hh // 2 if hh < 8 else 18 + hh // 2):
                        index_head(hh)
                        index_head(hh + 1)
                if k == P_A2 + 8:
                    evacuated(0, P_A3, [(t, th[:, t, NCOL:2 * NCOL], 0, NCOL) for t in range(TT)])
                if k == P_A3 + 8:
                    evacuated(1, P_A4, [(t, th[:, t, TH_KC:TH_KC + NCOL], 0, NCOL) for t in range(TT)])
                for kv in range(2):
                    if k == 28 + kv:
                        act.wait_ge(filled[BT], T_KC + kv)
                        s.activation(kvT[:, kv, :, :], aux[BT][:, :].rearrange("p (g t) -> p g t", g=GROUPS),
                                     ACT.Copy).then_inc(drained[BT], 1)
                    if k == 31 + kv:
                        act.wait_ge(xf_ready, 4 * (kv + 1))
                        s.activation(x_hi[:, kv * CLEN * NB:(kv + 1) * CLEN * NB],
                                     xf[:, kv, :, :].rearrange("p l n -> p (l n)"), ACT.Copy).then_inc(x_hi_ready, 1)
                for b, at, br, col in ((0, P_A4 + 8, 0, TH_KS), (1, P_A5 + 8, 1, TH_KW), (0, P_A6 + 8, 2, TH_DK)):
                    if k == at:
                        evacuated(b, at, [(t, th[:, t, col:col + 256], 0, 256) for t in range(TT)]
                                  + [(t, v_all[:, br, t, :, :], 256, 512) for t in range(TT)])
                for br, at, n in ((0, 39, T_KS), (1, 61, T_KW), (2, 69, T_DK)):
                    if k == at:
                        copied(BT, n, kT[:, br, :, :], aux[BT][:, :].rearrange("p (g t) -> p g t", g=GROUPS),
                               scale=k_gain[:, br + 1:br + 2])
                if k == P_W1K + 8:
                    hidden(0)
                if k == P_W1V + 8:
                    hidden(1)
                if k == 52:
                    copied(BT, T_HID, hidT[:, :, :], aux[BT][:, 0:4 * NB].rearrange("p (a n) -> p a n", a=4))
                if k == 54:
                    act.wait_ge(filled[BT], T_KC2)
                    s.activation(kc_nat[:, :], aux[BT][0:NB, 0:DH], ACT.Copy, scale=0.5).then_inc(kc_out, 1)
                    s.activation(vc[:, :, :], aux[BT][0:NC, DH:3 * DH].rearrange("p (g d) -> p g d", g=GROUPS), ACT.Copy,
                                 scale=0.5).then_inc(drained[BT], 1)
                if k == 56:
                    copied(BT, T_KCN, kcT[:, :], aux[BT][:, 0:NB], scale=k_gain[:, 0:1])

            def qz_out(n):
                act.wait_ge(piece_used, n * 16 + P_L)
                for t in range(TT):
                    s.activation(q_raw[:, t, :, :, :], acc[1][t][:, :].rearrange("p (m s d) -> p m s d", m=2, s=2), ACT.Copy,
                                 scale=rstd[:, t:t + 1]).then_inc(q_out if t == 0 else acc_out[1], 1)
                act.wait_ge(q_out, n + 1)
                act.wait_ge(acc_out[1], n + 5)
                s.activation(z_gate[:, :, :, :], q_raw[:, :, :, 1, :], ACT.Tanh, scale=0.5).then_inc(z_tanh, 1)

            def attend(k, i):
                if k == 3:
                    copied(BT, i * 5 + T_L, qT[:, :, :], aux[BT][:, :].rearrange("p (m t) -> p m t", m=2))
                if k == 4:
                    act.wait_ge(neg_ready, i * 2 + 1)
                    for t in range(TT):
                        s.activation(prob[:, 0, t * P:(2 * t + 1) * P], prob[:, 0, t * P:(2 * t + 1) * P], ACT.Exp,
                                     bias=neg_mx[:, 2 + t:3 + t], accum_out=rowsum[:, t, 1:2])
                    for t in range(TT):
                        e = s.activation(prob_c[:, t, :], prob_c[:, t, :], ACT.Exp, bias=neg_mx[:, t:t + 1],
                                         accum_out=rowsum[:, t, 0:1])
                    e.then_inc(exp_ready, 1)
                    for t in range(TT):
                        e = s.activation(prob[:, 1, t * P:(2 * t + 1) * P], prob[:, 1, t * P:(2 * t + 1) * P], ACT.Exp,
                                         bias=neg_mx[:, 4 + t:5 + t], accum_out=rowsum[:, t, 2:3])
                    e.then_inc(exp_ready, 1)
                if k == 5:
                    act.wait_ge(neg_ready, i * 2 + 2)
                    for t in range(TT):
                        e = s.activation(prob[:, 2, t * P:(2 * t + 1) * P], prob[:, 2, t * P:(2 * t + 1) * P], ACT.Exp,
                                         bias=neg_mx[:, 6 + t:7 + t], accum_out=rowsum[:, t, 3:4])
                    e.then_inc(exp_ready, 1)
                if k == 6:
                    copied(BT, i * 5 + T_L + 1, probT[:, 0, :], aux[BT][:, 0:3 * P])
                    copied(BO, i * 2 + O_L, prob_cT[:, :], aux[BO][0:NC, 0:T])
                if k == 7:
                    copied(BT, i * 5 + T_L + 2, probT[:, 1, :], aux[BT][:, 0:3 * P])
                if k == 8:
                    copied(BT, i * 5 + T_L + 3, probT[:, 2, :], aux[BT][:, 0:3 * P])
                if k == 8:
                    act.wait_ge(piece_used, i * 16 + P_L + 8)
                    for t in range(TT):
                        e = s.activation(th[:, t, bass.ds(i * NCOL, NCOL)], acc[0][t][:, :], ACT.Tanh, scale=half_rstd_x[:, t:t + 1])
                    e.then_inc(acc_out[0], 1)
                if k == 11:
                    act.wait_ge(filled[BT], i * 5 + T_L + 4)
                    s.activation(oT_hi[:, :, :].rearrange("p (m h) t -> p m h t", m=2)[:, :, bass.ds(i, 1), :].rearrange("p m h t -> p m (h t)"),
                                 aux[BT][:, :].rearrange("p (m t) -> p m t", m=2), ACT.Copy).then_inc(o_hi, 1)

            qz_out(0)
            with act.Fori(0, HEADS - 1) as i:
                for k in range(16):
                    rounded(P_L + k + AHEAD, i, 16)
                    attend(k, i)
                qz_out(i + 1)
            for k in range(8):
                rounded(P_L7 + k + AHEAD)
                attend(k, HEADS - 1)

            def yT_upper(j):
                for b, n in ((BT, T_Y), (BO, O_Y)):
                    act.wait_ge(filled[b], j + n)
                    s.activation(hT_hi[:, bass.ds(j * 4 + (0 if b == BT else 2), 2), :],
                                 aux[b][:, :].rearrange("p (k t) -> p k t", k=2), ACT.Copy).then_inc(y_hi, 1)

            def up_block(j, first):
                for k in range(8):
                    rounded(P_U + k + AHEAD, j, 8)
                    if k == 2 and not first:
                        yT_upper(j - 1)
                    if first:
                        attend(8 + k, HEADS - 1)

            up_block(0, True)
            with act.Fori(1, 4) as j:
                up_block(j, False)

            def embedded(q):
                col = D + q * NCOL
                if q % 2 == 0:
                    act.wait_ge(ple_made, q // 2 + 1)
                evacuated(1 - q % 2, P_PP + q + 1 if q % 2 else 0, [(t, th[:, t, col:col + NCOL], 0, NCOL) for t in range(TT)], scale=0.5)

            for k in range(4):
                rounded(P_PP + k + AHEAD)
                if k:
                    embedded(k - 1)
                if k == 2:
                    yT_upper(3)

            def x2T_upper(j):
                for b, n in ((BT, T_X), (BO, O_X)):
                    act.wait_ge(filled[b], n + j)
                    for q in range(2):
                        kt = 4 * j + q + (0 if b == BT else 2)
                        s.activation(oT_hi[:, kt, :], aux[b][:, q * T:(q + 1) * T], ACT.Copy,
                                     scale=vecT[:, V_PLE + kt:V_PLE + kt + 1]).then_inc(x2_hi, 1)

            for j in range(4):
                for k in range(8):
                    rounded(P_O + 8 * j + k + AHEAD)
                    if j == 0 and k == 0:
                        embedded(3)
                    if j and k == 3:
                        x2T_upper(j - 1)

            for j in range(4):
                for k in range(8):
                    if P_G + 8 * j + k + AHEAD < N_PIECES:
                        rounded(P_G + 8 * j + k + AHEAD)
                    if j == 0 and k == 3:
                        x2T_upper(3)
                b = (j + 1) % 2
                act.wait_ge(piece_used, P_G + 8 * j + 8)
                act.wait_ge(r2_ready, 1)
                if j:
                    act.wait_ge(out_ready, 2 * j)
                for t in range(TT):
                    e = s.activation(stage[:, t, :], acc[b][t][:, :], ACT.Tanh, scale=half_rstd[:, t:t + 1])
                    e.then_inc(g_tanh, 1)

        @block.vector
        def _(dve):
            v = nc.vector

            def rest(k0, i=0, per=0):
                dve.wait_ge(hi_ready, i * per + k0 + 1)
                n = 8 * N_SMALL if P_A0 <= k0 < P_A2 else 1024
                v.tensor_tensor(w_lo[:, k0 % RING, 0:n], raw[:, (k0 // 2) % RAW, k0 % 2, 0:n],
                                w_hi[:, k0 % RING, 0:n].bitcast(F32), ALU.subtract).then_inc(lo_ready, 1)

            dve.wait_ge(filled[BT], T_VEC)
            v.tensor_copy(vecT[:, :], aux[BT][:, 0:N_VEC]).then_inc(drained[BT], 1)
            dve.wait_ge(drained[BT], T_VEC)
            v.tensor_scalar(k_gain[:, 0:3], vecT[:, V_KC:V_KC + 3], vecT[:, V_NQ:V_NQ + 1], None, ALU.mult).then_inc(gain_ready, 1)
            v.tensor_tensor(k_gain[:, 3:4], vecT[:, V_DQ:V_DQ + 1], vecT[:, V_DK:V_DK + 1], ALU.mult).then_inc(gain_ready, 1)

            def hT_rest(u):
                b = (BT, BS0, BS1, BO)[u % 4]
                dve.wait_ge(t_hi, 2 * u + 2)
                for kt in (2 * u, 2 * u + 1):
                    e = v.scalar_tensor_tensor(out=hT_lo[:, kt, :], in0=aux[b][:, (kt % 2) * T:(kt % 2 + 1) * T],
                                               scalar=vecT[:, V_NORM + kt:V_NORM + kt + 1],
                                               in1=hT_hi[:, kt, :].bitcast(F32), op0=ALU.mult, op1=ALU.subtract)
                e.then_inc(drained[b], 1)

            def index_sum(hh):
                b = BS0 + hh % 2
                dve.wait_ge(drained[b], S_IDX + hh // 2)
                for t in range(TT):
                    part = slice(t * P, (2 * t + 1) * P)
                    w = th[:, t, TH_IW + hh:TH_IW + hh + 1]
                    if hh == 0:
                        v.tensor_scalar(score[:, part], rel[:, 0, part], w, None, ALU.mult).then_inc(scored, 1)
                    else:
                        dve.wait_ge(scored, 2 * hh - 1 + t)
                        v.scalar_tensor_tensor(out=score[:, part], in0=rel[:, hh % 2, part], scalar=w,
                                               in1=score[:, part], op0=ALU.mult, op1=ALU.add).then_inc(scored, 1)

            def topk_round(r):
                if r == 0:
                    dve.wait_ge(masked, 2)
                for t in range(TT):
                    part = slice(t * P, (2 * t + 1) * P)
                    if r:
                        dve.wait_ge(topk_step, 4 * r - 1 + t)
                    v.max(top8[:, t, :], work[:, part]).then_inc(topk_step, 1)
                for t in range(TT):
                    part = slice(t * P, (2 * t + 1) * P)
                    dve.wait_ge(topk_step, 4 * r + 1 + t)
                    v.match_replace(work[:, part], top8[:, t, :], work[:, part], TAKEN).then_inc(topk_step, 1)

            def k_squares(br, col):
                for t in range(TT):
                    for grp in range(GROUPS):
                        kk = th[:, t, col + grp * DH:col + (grp + 1) * DH]
                        v.tensor_tensor_reduce(th[:, t, 3328 + grp * DH:3328 + (grp + 1) * DH], kk, kk, 1.0, 0.0, ALU.mult,
                                               ALU.add, ssk[:, br, 2 * t + grp:2 * t + grp + 1]).then_inc(ss_k, 1)

            def k_normed(br, col):
                dve.wait_ge(rk_ready, br + 1)
                for t in range(TT):
                    for grp in range(GROUPS):
                        kk = th[:, t, col + grp * DH:col + (grp + 1) * DH]
                        v.tensor_scalar(kk, kk, rk[:, br, 2 * t + grp:2 * t + grp + 1], None, ALU.mult).then_inc(kn_ready, 1)

            for k in range(AHEAD):
                hT_rest(k)
                rest(k)
            for k in range(P_L):
                if k + AHEAD < KD // 2:
                    hT_rest(k + AHEAD)
                rest(k + AHEAD)
                if k == 3:
                    dve.wait_ge(x_first_in, 16)
                    dve.wait_ge(x_in, 16)
                    v.tensor_tensor_reduce(th[:, 1, D:2 * D], x_nat[:, 1, :], x_nat[:, 1, :], 1.0, 0.0, ALU.mult, ALU.add,
                                           ssx[:, 1:2]).then_inc(ss_x, 1)
                if k == P_A0:
                    dve.wait_ge(p_hi, 1)
                    v.tensor_tensor(pT_lo[:, :, :], aux[BT][:, :].rearrange("p (k t) -> p k t", k=2),
                                    pT_hi[:, :, :].bitcast(F32), ALU.subtract).then_inc(drained[BT], 1)
                if k == P_A2 + 4:
                    dve.wait_ge(ng_tanh, 1)
                    dve.wait_ge(masks, 12 + 2 * HEADS)
                    for t in range(TT):
                        v.tensor_scalar(gates[:, t, :, 0:3], tmp24[:, t, :].rearrange("p (h b) -> p h b", b=3), 0.25, 0.25,
                                        ALU.mult, ALU.add).then_inc(gates_step, 1)
                    for t in range(TT):
                        dve.wait_ge(gates_step, t + 1)
                        v.tensor_scalar(gates[:, t, :, 0], gates[:, t, :, 0], row_mask[:, t:t + 1], None,
                                        ALU.mult).then_inc(gates_ready, 1)
                for hh in range(0, IH, 2):
                    if k == (16 + hh // 2 if hh < 8 else 19 + hh // 2):
                        index_sum(hh)
                        index_sum(hh + 1)
                if 28 <= k < 28 + TOPK // 8:
                    topk_round(k - 28)
                if k == 36:
                    dve.wait_ge(topk_step, 4 * (TOPK // 8))
                    v.tensor_scalar(dist_dsa[:, :], work[:, :], 0.5 * TAKEN, FILL, ALU.is_gt, ALU.mult).then_inc(dsa_ready, 1)
                    dve.wait_ge(dsa_ready, 1)
                    v.tensor_tensor(dist_dsa[:, :], dist_dsa[:, :], dist[:, :], ALU.add).then_inc(dsa_ready, 1)
                for kv in range(2):
                    if k == 32 + kv:
                        dve.wait_ge(x_hi_ready, kv + 1)
                        part = slice(kv * CLEN * NB, (kv + 1) * CLEN * NB)
                        v.tensor_tensor(x_lo[:, part], xf[:, kv, :, :].rearrange("p l n -> p (l n)"),
                                        x_hi[:, part].bitcast(F32), ALU.subtract).then_inc(x_lo_ready, 1)
                    if k == (P_W1K, P_W1V)[kv] + 9:
                        dve.wait_ge(acc_out[1 - kv], 3 + kv)
                        v.scalar_tensor_tensor(out=hth[:, kv, :], in0=hth[:, kv, :], scalar=1.0, in1=hz[:, kv, :],
                                               op0=ALU.add, op1=ALU.mult).then_inc(hid_ready, 1)
                for br, at, b, n, col in ((0, 37, 0, 3, TH_KS), (1, 59, 1, 4, TH_KW), (2, 67, 0, 5, TH_DK)):
                    if k == at:
                        dve.wait_ge(acc_out[b], n)
                        if br:
                            dve.wait_ge(ss_k, 4 * br)
                        k_squares(br, col)
                    if k == at + 1:
                        k_normed(br, col)
                if k == 54:
                    dve.wait_ge(kc_out, 1)
                    v.tensor_tensor_reduce(kc_junk[:, :], kc_nat[:, :], kc_nat[:, :], 1.0, 0.0, ALU.mult, ALU.add,
                                           ssc[:, :]).then_inc(ss_c, 1)
                if k == 55:
                    dve.wait_ge(ss_c, 3)
                    v.tensor_scalar(kc_nat[:, :], kc_nat[:, :], rc[:, :], None, ALU.mult).then_inc(kcn_ready, 1)

            def fence(n):
                v.memset(fence_col[:, n:n + 1], 0.0)

            def scores(src, dist_ap, dst, m):
                return v.tensor_tensor_reduce(dst, src, dist_ap, slope[:, 0:1], -3e38, ALU.add, ALU.max, mx[:, m:m + 1])

            def attend(k, i):
                if k == 0:
                    dve.wait_ge(acc_out[1], i + 5)
                    dve.wait_ge(q_out, i + 1)
                    v.tensor_copy(slope[:, :], slopes[:, bass.ds(i, 1)]).then_inc(slope_ready, 1)
                    for t in range(TT):
                        for m in range(2):
                            qq = q_raw[:, t, m, 0, :]
                            v.tensor_tensor_reduce(q_n[:, t, m, :], qq, qq, 1.0, 0.0, ALU.mult, ALU.add,
                                                   ssq[:, 2 * t + m:2 * t + m + 1]).then_inc(ss_q, 1)
                if k == 1:
                    dve.wait_ge(rq_ready, i + 1)
                    for t in range(TT):
                        for m in range(2):
                            e = v.tensor_scalar(q_n[:, t, m, :], q_raw[:, t, m, 0, :], rq[:, 2 * t + m:2 * t + m + 1], None,
                                                ALU.mult)
                    e.then_inc(qn_ready, 1)
                if k == 2:
                    dve.wait_ge(z_tanh, i + 1)
                    for t in range(TT):
                        e = v.scalar_tensor_tensor(out=z_gate[:, t, :, :], in0=z_gate[:, t, :, :], scalar=1.0,
                                                   in1=q_raw[:, t, :, 1, :], op0=ALU.add, op1=ALU.mult)
                    e.then_inc(z_ready, 1)
                if k == 4:
                    dve.wait_ge(slope_ready, i + 1)
                    dve.wait_ge(filled[BS0], i * 2 + S_L)
                    fence(0)
                    for t in range(TT):
                        part = slice(t * P, (2 * t + 1) * P)
                        scores(aux[BS0][:, part], dist[:, part], prob[:, 0, part], 2 + t)
                    for t in range(TT):
                        e = scores(aux[BS0][:, 3 * P + t * 16:3 * P + t * 16 + NC], dist_c[:, t, :], prob_c[:, t, :], t)
                    e.then_inc(drained[BS0], 1)
                    dve.wait_ge(filled[BS1], i * 2 + S_L)
                    fence(1)
                    for t in range(TT):
                        part = slice(t * P, (2 * t + 1) * P)
                        e = scores(aux[BS1][:, part], dist[:, part], prob[:, 1, part], 4 + t)
                    e.then_inc(drained[BS1], 1)
                    dve.wait_ge(drained[BS1], i * 2 + S_L)
                    v.tensor_scalar(neg_mx[:, 0:6], mx[:, 0:6], -1.0, None, ALU.mult).then_inc(neg_ready, 1)
                if k == 5:
                    dve.wait_ge(filled[BS0], i * 2 + S_L + 1)
                    fence(2)
                    for t in range(TT):
                        part = slice(t * P, (2 * t + 1) * P)
                        e = scores(aux[BS0][:, part], dist_dsa[:, part], prob[:, 2, part], 6 + t)
                    e.then_inc(drained[BS0], 1)
                    dve.wait_ge(drained[BS0], i * 2 + S_L + 1)
                    v.tensor_scalar(neg_mx[:, 6:8], mx[:, 6:8], -1.0, None, ALU.mult).then_inc(neg_ready, 1)
                if k == 7:
                    dve.wait_ge(exp_ready, i * 3 + 3)
                    v.reciprocal(rrow[:, :, :], rowsum[:, :, :]).then_inc(coef_step, 1)
                    dve.wait_ge(coef_step, i + 1)
                    v.tensor_tensor(coef[:, :, :], rrow[:, :, :],
                                    gates[:, :, bass.ds(i, 1), :].rearrange("p t h b -> p t (h b)"), ALU.mult).then_inc(coef_ready, 1)
                    dve.wait_ge(coef_ready, i + 1)
                    dve.wait_ge(filled[BO], i * 2 + O_L + 1)
                    for t in range(TT):
                        v.tensor_scalar(o_nat[:, 0, t, :], aux[BO][:, t * P:(t + 1) * P], coef[:, t, 0:1], None,
                                        ALU.mult).then_inc(o_step, 1)
                    for t in range(TT):
                        dve.wait_ge(o_step, i * 2 + 1 + t)
                        e = v.scalar_tensor_tensor(out=o_nat[:, 0, t, :], in0=aux[BO][:, T + t * P:T + (t + 1) * P],
                                                   scalar=coef[:, t, 1:2], in1=o_nat[:, 0, t, :], op0=ALU.mult, op1=ALU.add)
                    e.then_inc(drained[BO], 1)
                if k == 9:
                    dve.wait_ge(filled[BS1], i * 2 + S_L + 1)
                    dve.wait_ge(z_ready, i + 1)
                    dve.wait_ge(drained[BO], i * 2 + O_L + 1)
                    for t in range(TT):
                        v.scalar_tensor_tensor(out=o_nat[:, 0, t, :], in0=aux[BS1][:, t * P:(t + 1) * P],
                                               scalar=coef[:, t, 2:3], in1=o_nat[:, 0, t, :], op0=ALU.mult, op1=ALU.add)
                    for t in range(TT):
                        e = v.scalar_tensor_tensor(out=o_nat[:, 1, t, :], in0=aux[BS1][:, T + t * P:T + (t + 1) * P],
                                                   scalar=coef[:, t, 3:4], in1=z_gate[:, t, 1, :], op0=ALU.mult,
                                                   op1=ALU.mult)
                    e.then_inc(drained[BS1], 1)
                    dve.wait_ge(drained[BS1], i * 2 + S_L + 1)
                    v.tensor_tensor(o_nat[:, 0, :, :], o_nat[:, 0, :, :], z_gate[:, :, 0, :], ALU.mult).then_inc(o_ready, 1)
                if k == 11:
                    dve.wait_ge(o_hi, i + 1)
                    head = [a[:, :, :].rearrange("p (m h) t -> p m h t", m=2)[:, :, bass.ds(i, 1), :].rearrange("p m h t -> p m (h t)")
                            for a in (oT_hi, oT_lo)]
                    e = v.tensor_tensor(head[1], aux[BT][:, :].rearrange("p (m t) -> p m t", m=2), head[0].bitcast(F32), ALU.subtract)
                    e.then_inc(drained[BT], 1)

            with dve.Fori(0, HEADS - 1) as i:
                for k in range(16):
                    rest(P_L + k + AHEAD, i, 16)
                    attend(k, i)
            for k in range(8):
                rest(P_L7 + k + AHEAD)
                attend(k, HEADS - 1)

            def yT_rest(j):
                for b, n, o in ((BT, 1, 0), (BO, 2, 2)):
                    dve.wait_ge(y_hi, j * 2 + n)
                    e = v.tensor_tensor(hT_lo[:, bass.ds(j * 4 + o, 2), :], aux[b][:, :].rearrange("p (k t) -> p k t", k=2),
                                        hT_hi[:, bass.ds(j * 4 + o, 2), :].bitcast(F32), ALU.subtract)
                    e.then_inc(drained[b], 1)

            def up_block(j, first):
                for k in range(8):
                    rest(P_U + k + AHEAD, j, 8)
                    if k == 2 and not first:
                        yT_rest(j - 1)
                    if first:
                        attend(8 + k, HEADS - 1)
                    if k == 6:
                        dve.wait_ge(piece_used, j * 8 + P_U + 6)
                        for t in range(TT):
                            g = th[:, t, bass.ds(j * NCOL, NCOL)]
                            e = v.scalar_tensor_tensor(out=g, in0=g, scalar=1.0, in1=acc[1][t][:, :], op0=ALU.add, op1=ALU.mult)
                        e.then_inc(acc_out[1], 1)
                dve.wait_ge(piece_used, j * 8 + P_U + 8)
                for t in range(TT):
                    g = th[:, t, bass.ds(j * NCOL + D, NCOL)]
                    e = v.scalar_tensor_tensor(out=g, in0=g, scalar=1.0, in1=acc[0][t][:, :], op0=ALU.add, op1=ALU.mult)
                e.then_inc(acc_out[0], 1)
                dve.wait_ge(acc_out[1], j + 13)
                dve.wait_ge(acc_out[0], j + 14)
                for t in range(TT):
                    e = v.tensor_tensor(stage[:, t, :], th[:, t, bass.ds(j * NCOL, NCOL)], th[:, t, bass.ds(j * NCOL + D, NCOL)],
                                        ALU.add)
                e.then_inc(y_ready, 1)

            up_block(0, True)
            with dve.Fori(1, 4) as j:
                up_block(j, False)
            for k in range(4):
                rest(P_PP + k + AHEAD)
                if k == 2:
                    yT_rest(3)

            def x2T_rest(j):
                for b, o in ((BT, 0), (BO, 2)):
                    dve.wait_ge(x2_hi, 4 * j + o + 2)
                    for q in range(2):
                        kt = 4 * j + o + q
                        e = v.scalar_tensor_tensor(out=oT_lo[:, kt, :], in0=aux[b][:, q * T:(q + 1) * T],
                                                   scalar=vecT[:, V_PLE + kt:V_PLE + kt + 1],
                                                   in1=oT_hi[:, kt, :].bitcast(F32), op0=ALU.mult, op1=ALU.subtract)
                    e.then_inc(drained[b], 1)

            for j in range(4):
                for k in range(8):
                    rest(P_O + 8 * j + k + AHEAD)
                    if j and k == 3:
                        x2T_rest(j - 1)
                b, n = (j + 1) % 2, (19, 20, 20, 21)[j]
                dve.wait_ge(piece_used, P_O + 8 * j + 8)
                if j == 0:
                    dve.wait_ge(xr_in, 32)
                for t in range(TT):
                    part = xr[:, t, j * NCOL:(j + 1) * NCOL]
                    e = v.scalar_tensor_tensor(out=part, in0=acc[b][t][:, :], scalar=0.5, in1=part, op0=ALU.mult, op1=ALU.add)
                e.then_inc(acc_out[b], 1)
                dve.wait_ge(acc_out[b], n)
                for t in range(TT):
                    part = xr[:, t, j * NCOL:(j + 1) * NCOL]
                    if j:
                        dve.wait_ge(x2_ss, 2 * j - 1 + t)
                    v.tensor_tensor_reduce(th[:, t, 0:NCOL], part, part, 1.0, 0.0, ALU.mult, ALU.add,
                                           ssp[:, t, j:j + 1]).then_inc(x2_ss, 1)

            for j in range(4):
                for k in range(8):
                    if P_G + 8 * j + k + AHEAD < N_PIECES:
                        rest(P_G + 8 * j + k + AHEAD)
                    if j == 0 and k == 3:
                        x2T_rest(3)
                b = (j + 1) % 2
                for t in range(TT):
                    dve.wait_ge(g_tanh, 2 * j + t + 1)
                    e = v.scalar_tensor_tensor(out=stage[:, t, :], in0=stage[:, t, :], scalar=1.0,
                                               in1=th[:, t, D + j * NCOL:D + (j + 1) * NCOL], op0=ALU.add, op1=ALU.mult)
                e.then_inc(acc_out[b], 1)
                dve.wait_ge(acc_out[b], (21, 22, 22, 23)[j])
                for t in range(TT):
                    part = xr[:, t, j * NCOL:(j + 1) * NCOL]
                    e = v.tensor_tensor(part, part, stage[:, t, :], ALU.add)
                    e.then_inc(out_ready, 1)

        @block.tensor
        def _(pe):
            m = nc.tensor

            def bank_free(b, n):
                if isinstance(n, int) and n <= 1:
                    return
                pe.wait_ge(drained[b], n - 1)

            def piece(k0, kts, hi, lo, b, first, last, width=NCOL, cols=NCOL, i=0, per=0, at=None):
                pe.wait_ge(lo_ready, i * per + k0 + 1)
                s = k0 % RING
                for q, kt in enumerate(kts):
                    c = at or q * width
                    wh, wl = w_hi[:, s, c:c + cols], w_lo[:, s, c:c + cols]
                    for t in range(TT):
                        o = acc[b][t][:, 0:cols]
                        st, en = first and q == 0, last and q == len(kts) - 1
                        xh, xl = hi[:, kt, t * P:(t + 1) * P], lo[:, kt, t * P:(t + 1) * P]
                        m.matmul(o, xh, wh, start=st, stop=False)
                        m.matmul(o, xh, wl, start=False, stop=False)
                        e = m.matmul(o, xl, wh, start=False, stop=en)
                if at is not None:
                    return e
                e.then_inc(piece_used, 1)

            def turned(b, n, sources):
                bank_free(b, n)
                at = 0
                for src in sources:
                    rows, w = src.shape[0], src.shape[-1]
                    e = m.transpose(aux[b][0:w, at:at + rows], src, ident[0:rows, 0:rows])
                    at += rows
                e.then_inc(filled[b], 1)

            pe.wait_ge(consts, 4)
            pe.wait_ge(vec_in, 160)
            m.transpose(aux[BT][:, 0:N_VEC], vecs[:, :], ident[0:N_VEC, 0:N_VEC]).then_inc(filled[BT], 1)

            def x_turned(u):
                b, n = (BT, BS0, BS1, BO)[u % 4], (2, 1, 1, 1)[u % 4] + u // 4
                turned(b, n, [x_nat[:, t, kt * P:(kt + 1) * P] for kt in (2 * u, 2 * u + 1) for t in range(TT)])

            def index_head(hh):
                b, part = BS0 + hh % 2, slice((hh % 2) * ID, (hh % 2 + 1) * ID)
                bank_free(b, S_IDX + hh // 2)
                for t in range(TT):
                    e = m.matmul(aux[b][:, t * P:(2 * t + 1) * P], iqT[part, hh // 2, t * P:(t + 1) * P],
                                 ikT[part, 0:(t + 1) * P], start=True, stop=True)
                e.then_inc(filled[b], 1)

            def compress(k0, kv):
                pe.wait_ge(lo_ready, k0 + 1)
                s = k0 % RING
                for q in range(4):
                    l = (k0 - (P_W1K, P_W1V)[kv]) * 4 + q
                    at = (kv * CLEN + l) * NB
                    wh, wl = w_hi[:, s, q * HID:(q + 1) * HID], w_lo[:, s, q * HID:(q + 1) * HID]
                    o = acc[1 - kv][kv][:, 0:HID]
                    m.matmul(o, x_hi[:, at:at + P], wh, start=(l == 0), stop=False)
                    m.matmul(o, x_hi[:, at:at + P], wl, start=False, stop=False)
                    e = m.matmul(o, x_lo[:, at:at + P], wh, start=False, stop=(l == CLEN - 1))
                e.then_inc(piece_used, 1)

            pe.wait_ge(x_first_in, 16)
            x_turned(0)
            x_turned(1)
            pe.wait_ge(x_in, 16)
            x_turned(2)
            x_turned(3)
            stages = [(P_A1, 0, 0), (P_A2, 0, 1), (P_A3, 1, 1), (P_A4, 0, 2), (P_A5, 1, 3), (P_A6, 0, 4), (P_Q0, 1, 4)]
            for k in range(P_L):
                if P_A0 <= k < P_A2:
                    h = k - P_A0
                    piece(k, range(8 * h, 8 * h + 8), hT_hi, hT_lo, 1, h == 0, h == 1, N_SMALL, N_SMALL)
                elif P_W1K <= k < P_A5:
                    kv = int(k >= P_W1V)
                    if k == P_W1K:
                        pe.wait_ge(x_lo_ready, 2)
                        pe.wait_ge(x_pad, 2)
                    if k in (P_W1K, P_W1V):
                        pe.wait_ge(acc_out[1 - kv], 2 + kv)
                    compress(k, kv)
                else:
                    for at, b, n in stages:
                        if at <= k < at + 8:
                            if k == at and n:
                                pe.wait_ge(acc_out[b], n)
                            if at == P_A1:
                                pe.wait_ge(drained[(BT, BS0, BS1, BO)[k % 4]], (2, 1, 1, 1)[k % 4] + k // 4)
                            piece(k, (2 * (k - at), 2 * (k - at) + 1), hT_hi, hT_lo, b, k == at, k == at + 7)
                if k < 4:
                    x_turned(k + 4)
                if k == 7:
                    pe.wait_ge(p_in, 16)
                    turned(BT, T_PLE, [p_nat[:, t, q * P:(q + 1) * P] for q in range(2) for t in range(TT)])
                if k == 11:
                    pe.wait_ge(acc_out[1], 1)
                    turned(BT, T_IK, [th[:, t, TH_IK2:TH_IK2 + P] for t in range(TT)])
                for u, at in enumerate((12, 13, 19, 20)):
                    if k == at:
                        pe.wait_ge(acc_out[0], 1 + u // 2)
                        turned(BT, T_IQ + u, [th[:, t, (2 * u + q) * P:(2 * u + q + 1) * P] for q in range(2) for t in range(TT)])
                for hh in range(0, IH, 2):
                    if k == (14 + hh // 2 if hh < 8 else 17 + hh // 2):
                        pe.wait_ge(drained[BT], T_IQ + (1 if hh < 8 else 3))
                        index_head(hh)
                        index_head(hh + 1)
                for kv in range(2):
                    if k == 27 + kv:
                        pe.wait_ge(acc_out[1], 2)
                        col = TH_KC + kv * 256
                        turned(BT, T_KC + kv, [th[:, t, col + grp * DH:col + (grp + 1) * DH]
                                               for grp in range(GROUPS) for t in range(TT)])
                for br, at, n, col in ((0, 38, T_KS, TH_KS), (1, 60, T_KW, TH_KW), (2, 68, T_DK, TH_DK)):
                    if k == at:
                        pe.wait_ge(kn_ready, 4 * (br + 1))
                        turned(BT, n, [th[:, t, col + grp * DH:col + (grp + 1) * DH] for grp in range(GROUPS) for t in range(TT)])
                if k == 51:
                    pe.wait_ge(hid_ready, 2)
                    turned(BT, T_HID, [hth[:, q // 2, (q % 2) * P:(q % 2 + 1) * P] for q in range(4)])
                if k == 53:
                    bank_free(BT, T_KC2)
                    pe.wait_ge(w2_in, 32)
                    for q in range(2):
                        m.matmul(aux[BT][0:NB, 0:DH], hidT[:, q, :], w2[:, 0, q, :], start=(q == 0), stop=(q == 1))
                    for grp in range(GROUPS):
                        for q in range(2):
                            e = m.matmul(aux[BT][0:NC, DH * (1 + grp):DH * (2 + grp)], hidT[:, 2 + q, grp * NC:(grp + 1) * NC],
                                         w2[:, 1, q, :], start=(q == 0), stop=(q == 1))
                    e.then_inc(filled[BT], 1)
                if k == 55:
                    pe.wait_ge(kcn_ready, 1)
                    turned(BT, T_KCN, [kc_nat[:, :]])

            def dots(b, mix, br, g):
                keys = kT[:, br, bass.ds(g, 1), :].rearrange("p g t -> p (g t)")
                for t in range(TT):
                    e = m.matmul(aux[b][:, t * P:(2 * t + 1) * P], qT[:, mix, t * P:(t + 1) * P],
                                 keys[:, 0:(t + 1) * P], start=True, stop=True)
                return e

            def probs_turned(n, br):
                bank_free(BT, n)
                for q in range(3):
                    e = m.transpose(aux[BT][:, q * P:(q + 1) * P], prob[:, br, q * P:(q + 1) * P], ident[:, :])
                e.then_inc(filled[BT], 1)

            def weighted(b, at, br, g):
                vals = [v_all[:, br, kt, bass.ds(g, 1), :].rearrange("p g d -> p (g d)") for kt in range(TT)]
                m.matmul(aux[b][:, at:at + P], probT[:, br, 0:P], vals[0], start=True, stop=True)
                m.matmul(aux[b][:, at + P:at + 2 * P], probT[:, br, P:2 * P], vals[0], start=True, stop=False)
                return m.matmul(aux[b][:, at + P:at + 2 * P], probT[:, br, 2 * P:3 * P], vals[1], start=False, stop=True)

            def attend(k, i):
                g = i // 4
                nT = i * 5 + T_L
                if k == 2:
                    pe.wait_ge(qn_ready, i + 1)
                    bank_free(BT, nT)
                    for mix in range(2):
                        for t in range(TT):
                            e = m.transpose(aux[BT][:, mix * T + t * P:mix * T + (t + 1) * P], q_n[:, t, mix, :], ident[:, :])
                    e.then_inc(filled[BT], 1)
                if k == 3:
                    pe.wait_ge(drained[BT], nT)
                    bank_free(BS0, i * 2 + S_L)
                    dots(BS0, 0, 0, g)
                    ck = kcT[:, bass.ds(g * NC, NC)]
                    for t in range(TT):
                        e = m.matmul(aux[BS0][:, 3 * P + t * 16:3 * P + t * 16 + NC], qT[:, 0, t * P:(t + 1) * P], ck,
                                     start=True, stop=True)
                    e.then_inc(filled[BS0], 1)
                    bank_free(BS1, i * 2 + S_L)
                    dots(BS1, 0, 1, g).then_inc(filled[BS1], 1)
                if k == 4:
                    bank_free(BS0, i * 2 + S_L + 1)
                    dots(BS0, 1, 2, g).then_inc(filled[BS0], 1)
                if k == 5:
                    pe.wait_ge(exp_ready, i * 3 + 1)
                    probs_turned(nT + 1, 0)
                    bank_free(BO, i * 2 + O_L)
                    for t in range(TT):
                        e = m.transpose(aux[BO][0:NC, t * P:(t + 1) * P], prob_c[:, t, :], ident[:, :])
                    e.then_inc(filled[BO], 1)
                if k == 6:
                    pe.wait_ge(exp_ready, i * 3 + 2)
                    probs_turned(nT + 2, 1)
                    bank_free(BO, i * 2 + O_L + 1)
                    cv = vc[:, bass.ds(g, 1), :].rearrange("p g d -> p (g d)")
                    for t in range(TT):
                        m.matmul(aux[BO][:, t * P:(t + 1) * P], prob_cT[:, t * P:(t + 1) * P], cv, start=True, stop=True)
                    weighted(BO, T, 0, g).then_inc(filled[BO], 1)
                if k == 7:
                    pe.wait_ge(exp_ready, i * 3 + 3)
                    probs_turned(nT + 3, 2)
                    bank_free(BS1, i * 2 + S_L + 1)
                    weighted(BS1, 0, 1, g)
                if k == 8:
                    pe.wait_ge(drained[BT], nT + 3)
                    weighted(BS1, T, 2, g).then_inc(filled[BS1], 1)
                if k == 10:
                    pe.wait_ge(o_ready, i + 1)
                    bank_free(BT, nT + 4)
                    for mix in range(2):
                        for t in range(TT):
                            e = m.transpose(aux[BT][:, mix * T + t * P:mix * T + (t + 1) * P], o_nat[:, mix, t, :], ident[:, :])
                    e.then_inc(filled[BT], 1)

            with pe.Fori(0, HEADS - 1) as i:
                for k in range(8):
                    if k == 0:
                        pe.wait_ge(acc_out[0], i + 5)
                    piece(P_L + k, (2 * k, 2 * k + 1), hT_hi, hT_lo, 0, k == 0, k == 7, i=i, per=16)
                    attend(k, i)
                pe.wait_ge(acc_out[1], i + 5)
                for k in range(8):
                    piece(P_L + 8 + k, (2 * k, 2 * k + 1), hT_hi, hT_lo, 1, k == 0, k == 7, i=i, per=16)
                    attend(8 + k, i)
            pe.wait_ge(acc_out[0], HEADS + 4)
            for k in range(8):
                piece(P_L7 + k, (2 * k, 2 * k + 1), hT_hi, hT_lo, 0, k == 0, k == 7)
                attend(k, HEADS - 1)

            def y_turned(j):
                pe.wait_ge(y_ready, j + 1)
                for b, n, o in ((BT, T_Y, 0), (BO, O_Y, 2)):
                    bank_free(b, j + n)
                    for q in range(2):
                        for t in range(TT):
                            e = m.transpose(aux[b][:, q * T + t * P:q * T + (t + 1) * P],
                                            stage[:, t, (o + q) * P:(o + q + 1) * P], ident[:, :])
                    e.then_inc(filled[b], 1)

            def up_block(j, first):
                for k in range(8):
                    b, half = 1 - k // 2 % 2, k // 4
                    if k == 0:
                        pe.wait_ge(acc_out[1], j + 12)
                    if k == 2:
                        pe.wait_ge(acc_out[0], j + 13)
                    if k == 4 and first:
                        pe.wait_ge(drained[BT], T_Y - 1)
                    kt = (1 - b) * HEADS + 4 * half + 2 * (k % 2)
                    piece(P_U + k, (kt, kt + 1), oT_hi, oT_lo, b, k in (0, 2), k in (5, 7), i=j, per=8)
                    if k == 1 and not first:
                        y_turned(j - 1)
                    if first:
                        attend(8 + k, HEADS - 1)

            up_block(0, True)
            with pe.Fori(1, 4) as j:
                up_block(j, False)
            for k in range(4):
                pe.wait_ge(acc_out[1 - k % 2], (16, 17)[k % 2] + k // 2)
                for kt in range(2):
                    e = piece(P_PP + k // 2 * 2 + kt, (kt,), pT_hi, pT_lo, 1 - k % 2, kt == 0, kt == 1, at=k % 2 * NCOL)
                    if k % 2:
                        e.then_inc(piece_used, 1)
                    elif kt:
                        e.then_inc(ple_made, 1)
                if k == 1:
                    y_turned(3)

            def x2_turned(j):
                pe.wait_ge(acc_out[(j + 1) % 2], (19, 20, 20, 21)[j])
                for b, n, o in ((BT, T_X, 0), (BO, O_X, 2)):
                    bank_free(b, j + n)
                    for q in range(2):
                        for t in range(TT):
                            c = j * NCOL + (o + q) * P
                            e = m.transpose(aux[b][:, q * T + t * P:q * T + (t + 1) * P], xr[:, t, c:c + P], ident[:, :])
                    e.then_inc(filled[b], 1)

            for j in range(4):
                b, n = (j + 1) % 2, (18, 19, 19, 20)[j]
                pe.wait_ge(acc_out[b], n)
                for k in range(8):
                    if j == 0:
                        pe.wait_ge(drained[(BT, BO)[k % 2]], (T_Y, O_Y)[k % 2] + k // 2)
                    piece(P_O + 8 * j + k, (2 * k, 2 * k + 1), hT_hi, hT_lo, b, k == 0, k == 7)
                    if j and k == 2:
                        x2_turned(j - 1)
            for j in range(4):
                b, n = (j + 1) % 2, (20, 21, 21, 22)[j]
                pe.wait_ge(acc_out[b], n)
                for k in range(8):
                    if j == 0:
                        pe.wait_ge(drained[(BT, BO)[k % 2]], (T_X, O_X)[k % 2] + k // 2)
                    piece(P_G + 8 * j + k, (2 * k, 2 * k + 1), oT_hi, oT_lo, b, k == 0, k == 7)
                    if j == 0 and k == 2:
                        x2_turned(3)


_INS = ["x", "p", "norm_g", "w_in", "nsa_q_g", "nsa_kc_g", "nsa_ks_g", "nsa_kw_g", "cmp_pe_k", "cmp_w1_k", "cmp_w2_k",
        "cmp_pe_v", "cmp_w1_v", "cmp_w2_v", "dsa_q_g", "dsa_k_g", "w_up_nsa", "w_up_dsa", "w_out", "ple_norm_g",
        "w_ple_gate", "w_ple_proj"]
_OUTS = [((1, T, D), "float32")]


def kernel(**inputs):
    import numpy as _np
    import concourse.bacc as _bacc
    from concourse import mybir as _mybir
    from concourse.bass_utils import run_bass_kernel_spmd as _run

    nc = _bacc.Bacc("TRN2", target_bir_lowering=False, num_devices=1)
    arrays, args = {}, []
    for name in _INS:
        a = _np.ascontiguousarray(inputs[name])
        arrays[f"in_{name}_dram"] = a
        args.append(nc.dram_tensor(f"in_{name}_dram", a.shape, _mybir.dt.from_np(a.dtype), kind="ExternalInput").ap())
    for i, (shape, dtype) in enumerate(_OUTS):
        dt = _mybir.dt.from_np(_np.dtype(dtype))
        args.append(nc.dram_tensor(f"out_{i}_dram", shape, dt, kind="ExternalOutput").ap())
    build(nc, *args)
    r = _run(nc, [arrays], core_ids=[0])
    got = tuple(r.results[0][f"out_{i}_dram"] for i in range(len(_OUTS)))
    return got[0]
```

```python
from contextlib import ExitStack

import concourse.bass as bass
from concourse import mybir

F32 = mybir.dt.float32
F32R = mybir.dt.float32r
ALU = mybir.AluOpType
ACT = mybir.ActivationFunctionType

P = 128
D = 2048
T = 256
TT = T // P
KD = D // P
HEADS = 8
DH = 128
GROUPS = 2
HID = 256
CLEN, CSTR = 32, 16
NC = (T - CLEN) // CSTR + 1
NB = GROUPS * NC
IH, ID = 16, 64
TOPK = T // 4
NCOL = 512
EPS = 1e-6
FILL = -1e34
NEG = -1e30
TAKEN = -3e38

C_NQ, C_KC, C_KS, C_KW, C_NG, C_NZ = 0, 1024, 1536, 2048, 2560, 2584
C_DQ, C_DK, C_IQ, C_IK, C_DZ, C_MG = 3608, 4632, 5144, 6168, 6248, 7272
N_SMALL = 24 + 80

TH_KC, TH_KS, TH_KW, TH_DK, TH_NG, TH_IK, TH_IW, TH_IK2, TH_SMALL, TH_HID = 1024, 1536, 2048, 2560, 3072, 3096, 3160, 3200, 3600, 3600

P_A1, P_A0, P_A2, P_A3, P_A4, P_MIX, P_Q0 = 0, 8, 10, 18, 26, 34, 66
P_L = 74
P_L7 = P_L + 16 * (HEADS - 1)
P_U = P_L7 + 8
P_PP = P_U + 32
P_O = P_PP + 4
P_G = P_O + 32
N_PIECES = P_G + 32
ACC_L = 4
TOPK_AT = (29, 30, 31, 32, 33, 36, 37, 40)
AHEAD = 2
RAW, RING = 4, 4

X_PARTS = (0, 256, 512, 1024, 2048)

V_NORM, V_PLE, V_NQ, V_KC, V_KS, V_KW, V_DQ, V_DK, V_PEK, V_PEV = 0, 16, 32, 33, 34, 35, 36, 37, 38, 70
N_VEC = 102

BT, BS0, BS1, BO = 0, 1, 2, 3
T_NORM, T_PLE, T_VEC, T_SMALL, T_IK, T_IQ, T_KC, T_VC, T_KS, T_HK, T_KW, T_KC2, T_KCN, T_HV, T_DK, T_VC2 = (
    1, 4, 5, 6, 7, 8, 12, 13, 14, 15, 16, 17, 18, 19, 20, 21)
T_L, T_Y, T_X = 22, 62, 66
X_BANKS, X_USES = (BO, BS0, BS1, BT), (1, 1, 1, 2)
S_IDX, S_W1, S_L = 3, 11, 12
O_L, O_Y, O_X = 3, 19, 23


def build(nc, x, p, norm_g, w_in, nsa_q_g, nsa_kc_g, nsa_ks_g, nsa_kw_g, cmp_pe_k, cmp_w1_k, cmp_w2_k,
          cmp_pe_v, cmp_w1_v, cmp_w2_v, dsa_q_g, dsa_k_g, w_up_nsa, w_up_dsa, w_out, ple_norm_g,
          w_ple_gate, w_ple_proj, out):
    ctx = ExitStack()

    def sb(name, shape, dt=F32, stack=None):
        return (stack or ctx).enter_context(nc.sbuf_tensor(name, shape, dt))

    def sem(name):
        return ctx.enter_context(nc.semaphore(name))

    with ctx:
        raw = sb("raw", [P, RAW, 2, 1024])
        w_hi = sb("w_hi", [P, RING, 1024], F32R)
        w_lo = sb("w_lo", [P, RING, 1024], F32R)
        hT_hi = sb("hT_hi", [P, KD, T], F32R)
        hT_lo = sb("hT_lo", [P, KD, T], F32R)
        th = sb("th", [P, TT, 2 * D])
        kT = sb("kT", [P, 3, GROUPS, T])
        v_all = sb("v_all", [P, 3, TT, GROUPS, DH])
        kcT = sb("kcT", [P, NB])
        vc = sb("vc", [NC, GROUPS, DH])
        dist = sb("dist", [P, 3 * P])
        dist_dsa = sb("dist_dsa", [P, 3 * P])
        dist_c = sb("dist_c", [P, TT, NC])
        ident = sb("ident", [P, P])
        normT = sb("normT", [P, KD])
        vecT = sb("vecT", [P, N_VEC])
        k_gain = sb("k_gain", [P, 4])
        slopes = sb("slopes", [P, HEADS])
        inv_slopes = sb("inv_slopes", [P, HEADS, 4])
        slope = sb("slope", [P, 1])
        warm = sb("warm", [P, 1])
        fence_col = sb("fence_col", [P, 3])
        m_half = sb("m_half", [P, 16])
        q_eps = sb("q_eps", [P, 4])
        row_mask = sb("row_mask", [P, TT])
        gates = sb("gates", [P, TT, HEADS, 4])
        pT_hi = sb("pT_hi", [P, 2, T], F32R)
        pT_lo = sb("pT_lo", [P, 2, T], F32R)
        ssx = sb("ssx", [P, TT])
        rstd = sb("rstd", [P, TT])
        half_rstd_x = sb("half_rstd_x", [P, TT])
        ssk = sb("ssk", [P, 3, 4])
        rk = sb("rk", [P, 3, 4])
        ssc = sb("ssc", [NB, 1])
        rc = sb("rc", [NB, 1])
        ssq = sb("ssq", [P, 4])
        rq = sb("rq", [P, 4])
        mx = sb("mx", [P, 8])
        neg_mx = sb("neg_mx", [P, 8])
        rowsum = sb("rowsum", [P, TT, 4])
        rrow = sb("rrow", [P, TT, 4])
        coef = sb("coef", [P, TT, 4])
        ssp = sb("ssp", [P, TT, 4])
        ssp2 = sb("ssp2", [P, TT])
        half_rstd = sb("half_rstd", [P, TT])

        with ExitStack() as st:
            x_nat = sb("x_nat", [P, TT, D], stack=st)
        with ExitStack() as st:
            kvT = sb("kvT", [P, 2, GROUPS, T], stack=st)
            xf = sb("xf", [P, 2, CLEN, NB], stack=st)
            x_hl = sb("x_hl", [P, 2 * CLEN * 2 * NB + P - 2 * NB], F32R, stack=st)
        oT_hi = sb("oT_hi", [P, 2 * HEADS, T], F32R)
        oT_lo = sb("oT_lo", [P, 2 * HEADS, T], F32R)

        with ExitStack() as st:
            iqT = sb("iqT", [P, IH // 2, T], stack=st)
            ikT = sb("ikT", [P, T], stack=st)
            rel = sb("rel", [P, 2, 3 * P], stack=st)
            score = sb("score", [P, 3 * P], stack=st)
            work = sb("work", [P, 3 * P], stack=st)
            top8 = sb("top8", [P, TT, 8], stack=st)
            tmp24 = sb("tmp24", [P, TT, 24], stack=st)
            p_nat = sb("p_nat", [P, TT, 256], stack=st)
            vecs = sb("vecs", [N_VEC, P], stack=st)
            hz = sb("hz", [NB, 2, HID], stack=st)
            hth = sb("hth", [NB, 2, HID], stack=st)
            hidT = sb("hidT", [P, 4, NB], stack=st)
            kc_nat = sb("kc_nat", [NB, DH], stack=st)
            kc_junk = sb("kc_junk", [NB, DH], stack=st)
            w2 = sb("w2", [P, 2, 2, DH], stack=st)
        with ExitStack() as st:
            q_raw = sb("q_raw", [P, TT, 2, 2, P], stack=st)
            z_gate = sb("z_gate", [P, TT, 2, P], stack=st)
            q_n = sb("q_n", [P, TT, 2, P], stack=st)
            qT = sb("qT", [P, 2, T], stack=st)
            prob = sb("prob", [P, 3, 3 * P], stack=st)
            prob_c = sb("prob_c", [P, TT, NC], stack=st)
            probT = sb("probT", [P, 3, 3 * P], stack=st)
            prob_cT = sb("prob_cT", [NC, T], stack=st)
            o_nat = sb("o_nat", [P, 2, TT, P], stack=st)
        xr = sb("xr", [P, TT, D])
        stage = sb("stage", [P, TT, NCOL])

        acc = [[ctx.enter_context(nc.psum_tensor(f"acc{b}{t}", [P, NCOL], F32)) for t in range(TT)] for b in range(2)]
        aux = [ctx.enter_context(nc.psum_tensor(n, [P, 512], F32)) for n in ("aux_t", "aux_s0", "aux_s1", "aux_o")]

        norm_in, vec_in, p_in, w2_in, xr_in, stored = (sem(n) for n in ("norm_in", "vec_in", "p_in", "w2_in", "xr_in", "stored"))
        x_in = [sem(f"x_in{c}") for c in range(len(X_PARTS) - 1)]
        piece0_in = sem("piece0_in")
        landed = [sem(f"landed{s}") for s in range(RAW)]
        hi_ready, lo_ready, piece_used = sem("hi_ready"), sem("lo_ready"), sem("piece_used")
        acc_out = [sem(f"acc_out{b}") for b in range(2)]
        filled = [sem(f"filled_{n}") for n in ("t", "s0", "s1", "o")]
        drained = [sem(f"drained_{n}") for n in ("t", "s0", "s1", "o")]
        consts, masks, ss_x, rstd_ready = (sem(n) for n in ("consts", "masks", "ss_x", "rstd_ready"))
        gain_ready, t_hi = sem("gain_ready"), sem("t_hi")
        p_hi, ng_tanh, gates_ready, gates_step = (sem(n) for n in ("p_hi", "ng_tanh", "gates_ready", "gates_step"))
        scored, masked, topk_step, dsa_ready = (sem(n) for n in ("scored", "masked", "topk_step", "dsa_ready"))
        ss_k, rk_step, rk_ready, kn_ready = (sem(n) for n in ("ss_k", "rk_step", "rk_ready", "kn_ready"))
        xf_ready, x_hi_ready, x_lo_ready, x_pad = (sem(n) for n in ("xf_ready", "x_hi_ready", "x_lo_ready", "x_pad"))
        hid_out, hid_ready, ss_c, kcn_ready = (sem(n) for n in ("hid_out", "hid_ready", "ss_c", "kcn_ready"))
        q_out, z_tanh, ss_q, rq_step, rq_ready, qn_ready, z_ready, slope_ready = (
            sem(n) for n in ("q_out", "z_tanh", "ss_q", "rq_step", "rq_ready", "qn_ready", "z_ready", "slope_ready"))
        neg_ready, exp_ready, coef_step, coef_ready, o_step, o_ready, o_hi = (
            sem(n) for n in ("neg_ready", "exp_ready", "coef_step", "coef_ready", "o_step", "o_ready", "o_hi"))
        y_ready, y_hi, ple_made = sem("y_ready"), sem("y_hi"), sem("ple_made")
        first_tile_done, gated = sem("first_tile_done"), sem("gated")
        x2_ss, ss2_step, r2_ready, x2_hi = (sem(n) for n in ("x2_ss", "ss2_step", "r2_ready", "x2_hi"))
        g_tanh, out_ready = sem("g_tanh"), sem("out_ready")

        n_dmas = {P_A0 // 2: 4}
        for c in range(P_Q0 // 2, P_L // 2):
            n_dmas[c] = 4
        for h in range(HEADS - 1):
            for c in range(P_L // 2 + 8 * h + 4, P_L // 2 + 8 * h + 8):
                n_dmas[c] = 4
        landed_at, count = [], [0] * RAW
        for c in range(N_PIECES // 2):
            count[c % RAW] += 16 * n_dmas.get(c, 1)
            landed_at.append(count[c % RAW])

        def wait_landed(eng, c, i=0, per=0):
            step = landed_at[c + per] - landed_at[c] if per else 0
            eng.wait_ge(landed[c % RAW], i * step + landed_at[c])

        x_split = x_hl[:, 0:2 * CLEN * 2 * NB].rearrange("p (a l s n) -> p a l s n", a=2, l=CLEN, s=2)

        block = ctx.enter_context(nc.Block())

        @block.sync
        def _(sp):
            def load_x(c):
                part = slice(X_PARTS[c], X_PARTS[c + 1])
                sp.dma_start(x_nat[:, :, part], x[0, :, part].rearrange("(t p) n -> p t n", p=P)).then_inc(x_in[c], 16)

            def slot_free(c, i=0, per=0):
                if c >= RAW:
                    sp.wait_ge(lo_ready, i * 2 * per + 2 * (c - RAW) + 2)

            def load(c, src, i=0, per=0):
                slot_free(c, i, per)
                sp.dma_start(raw[:, c % RAW, :, :].rearrange("p a (k n) -> p (a k) n", n=NCOL),
                             src.rearrange("(k p) n -> p k n", p=P)).then_inc(landed[c % RAW], 16)

            def load_block(c0, w, col, i=0, per=0):
                for q in range(4):
                    load(c0 + q, w[q * 4 * P:(q + 1) * 4 * P, col], i, per)

            def load_qz(c0, h, i=0, per=0):
                for q in range(4):
                    c = c0 + q
                    slot_free(c, i, per)
                    rows = w_in[0, q * 4 * P:(q + 1) * 4 * P, :]
                    dst = raw[:, c % RAW, :, :].rearrange("p a (k s n) -> p (a k) s n", s=4, n=P)
                    for s, col in enumerate((C_NQ, C_NZ, C_DQ, C_DZ)):
                        sp.dma_start(dst[:, :, s, :], rows[:, bass.ds(h * P + col, P)].rearrange("(k p) n -> p k n", p=P)
                                     ).then_inc(landed[c % RAW], 16)

            def load_vectors(rows, arrays, done):
                for v in arrays:
                    sp.dma_start(vecs[rows:rows + v.shape[0], :], v).then_inc(done, 16)
                    rows += v.shape[0]

            wi = w_in[0]
            for a in range(2):
                load_x(a)
                if a == 0:
                    load_vectors(V_NORM, [norm_g[0].rearrange("(a b) -> a b", b=P)], norm_in)
                sp.dma_start(raw[:, 0, a, :].rearrange("p (k n) -> p k n", n=NCOL),
                             wi[2 * a * P:2 * (a + 1) * P, C_IQ:C_IQ + NCOL].rearrange("(k p) n -> p k n", p=P)
                             ).then_inc(landed[0] if a else piece0_in, 16)
            for c in range(1, 4):
                if c < 3:
                    load_x(c + 1)
                load(c, wi[c * 4 * P:(c + 1) * 4 * P, C_IQ:C_IQ + NCOL])
            load_vectors(V_PLE, [ple_norm_g[0].rearrange("(a b) -> a b", b=P), nsa_q_g, nsa_kc_g, nsa_ks_g, nsa_kw_g,
                                 dsa_q_g, dsa_k_g, cmp_pe_k[0], cmp_pe_v[0]], vec_in)
            sp.dma_start(p_nat[:, :, :], p[0, 0].rearrange("(t p) n -> p t n", p=P)).then_inc(p_in, 16)
            c = P_A0 // 2
            slot_free(c)
            for half in range(2):
                dst = raw[:, c % RAW, half, 0:8 * N_SMALL].rearrange("p (k n) -> p k n", n=N_SMALL)
                rows = wi[half * 8 * P:(half + 1) * 8 * P, :].rearrange("(k p) n -> p k n", p=P)
                sp.dma_start(dst[:, :, 0:24], rows[:, :, C_NG:C_NG + 24]).then_inc(landed[c % RAW], 16)
                sp.dma_start(dst[:, :, 24:N_SMALL], rows[:, :, C_IK:C_IK + 80]).then_inc(landed[c % RAW], 16)
            for kv, w in enumerate((cmp_w2_k, cmp_w2_v)):
                sp.dma_start(w2[:, kv, :, :], w[0].rearrange("(k p) n -> p k n", p=P)).then_inc(w2_in, 16)
            load_block(P_A2 // 2, wi, slice(C_IQ + NCOL, C_IQ + 2 * NCOL))
            load_block(P_A3 // 2, wi, slice(C_KC, C_KC + NCOL))
            load_block(P_A4 // 2, wi, slice(C_KS, C_KS + NCOL))
            for m in range(8):
                c, q = P_MIX // 2 + 2 * m, m % 4
                slot_free(c)
                w1, col = ((cmp_w1_k, C_KW), (cmp_w1_v, C_DK))[m // 4]
                sp.dma_start(raw[:, c % RAW, :, :].rearrange("p a (k n) -> p (a k) n", n=HID),
                             w1[0, q * 8 * P:(q + 1) * 8 * P, :].rearrange("(k p) n -> p k n", p=P)
                             ).then_inc(landed[c % RAW], 16)
                load(c + 1, wi[q * 4 * P:(q + 1) * 4 * P, col:col + NCOL])
            load_qz(P_Q0 // 2, 0)
            with sp.Fori(0, HEADS - 1) as i:
                load_block(P_L // 2, wi, bass.ds(i * NCOL + C_MG, NCOL), i, 8)
                load_qz(P_L // 2 + 4, i + 1, i, 8)
            load_block(P_L7 // 2, wi, slice(C_MG + 7 * NCOL, C_MG + 8 * NCOL))
            with sp.Fori(0, 4) as j:
                for q in range(2):
                    for b, w in enumerate((w_up_nsa, w_up_dsa)):
                        load(P_U // 2 + 2 * q + b, w[0, q * 4 * P:(q + 1) * 4 * P, bass.ds(j * NCOL, NCOL)], j, 4)
            for q in range(2):
                c = P_PP // 2 + q
                slot_free(c)
                sp.dma_start(raw[:, c % RAW, :, :], w_ple_proj[0, :, q * 2 * NCOL:(q + 1) * 2 * NCOL].rearrange(
                    "(k p) n -> p k n", p=P)).then_inc(landed[c % RAW], 16)
            sp.wait_ge(drained[BT], T_Y - 1)
            for t in range(TT):
                sp.dma_start(xr[:, t, :], x[0, t * P:(t + 1) * P, :]).then_inc(xr_in, 16)
            with sp.Fori(0, 4) as j:
                load_block(P_O // 2, w_out[0], bass.ds(j * NCOL, NCOL), j, 4)
            with sp.Fori(0, 4) as j:
                load_block(P_G // 2, w_ple_gate[0], bass.ds(j * NCOL, NCOL), j, 4)
            for j in range(4):
                for t in range(TT):
                    sp.wait_ge(out_ready, 2 * j + t + 1)
                    sp.dma_start(out[0, t * P:(t + 1) * P, j * NCOL:(j + 1) * NCOL],
                                 xr[:, t, j * NCOL:(j + 1) * NCOL]).then_inc(stored, 16)
            sp.wait_ge(stored, 16 * 8)

        @block.gpsimd
        def _(pool):
            g = nc.gpsimd
            g.memset(ident[:, :], 0.0).then_inc(consts, 1)
            g.memset(m_half[:, :], -0.5).then_inc(consts, 1)
            g.memset(q_eps[:, :], DH * EPS).then_inc(consts, 1)
            pool.wait_ge(consts, 3)
            g.affine_select(out=ident[:, :], in_=ident[:, :], compare_op=ALU.not_equal, fill=1.0, base=0,
                            pattern=[[-1, P]], channel_multiplier=1).then_inc(consts, 1)

            pool.wait_ge(ss_x, 2)
            g.tensor_scalar(rstd[:, :], ssx[:, :], 1.0 / D, EPS, ALU.mult, ALU.add).then_inc(rstd_ready, 1)
            pool.wait_ge(rstd_ready, 1)
            g.tensor_tensor(rstd[:, :], rstd[:, :], m_half[:, 0:TT], ALU.pow).then_inc(rstd_ready, 1)
            pool.wait_ge(rstd_ready, 2)
            g.tensor_scalar(half_rstd_x[:, :], rstd[:, :], 0.5, None, ALU.mult).then_inc(rstd_ready, 1)

            g.iota(dist[:, 0:P], pattern=[[1, P]], base=0, channel_multiplier=-1,
                   allow_small_or_imprecise_dtypes=True).then_inc(masks, 1)
            g.iota(dist[:, P:], pattern=[[1, T]], base=-P, channel_multiplier=-1,
                   allow_small_or_imprecise_dtypes=True).then_inc(masks, 1)
            for t in range(TT):
                g.iota(dist_c[:, t, :], pattern=[[CSTR, NC]], base=-P * t, channel_multiplier=-1,
                       allow_small_or_imprecise_dtypes=True).then_inc(masks, 1)
            g.memset(row_mask[:, :], 1.0).then_inc(masks, 1)
            for h in range(HEADS):
                g.memset(slopes[:, h:h + 1], 2.0 ** -(h + 1)).then_inc(masks, 1)
                g.memset(inv_slopes[:, h, :], 2.0 ** (h + 1)).then_inc(masks, 1)
            g.memset(gates[:, :, :, 3], 0.5).then_inc(masks, 1)
            pool.wait_ge(masks, 6 + 2 * HEADS)
            g.affine_select(out=dist[:, 0:P], in_=dist[:, 0:P], compare_op=ALU.is_ge, fill=FILL, base=0,
                            pattern=[[-1, P]], channel_multiplier=1).then_inc(masks, 1)
            g.affine_select(out=dist[:, P:], in_=dist[:, P:], compare_op=ALU.is_ge, fill=FILL, base=P,
                            pattern=[[-1, T]], channel_multiplier=1).then_inc(masks, 1)
            g.tensor_scalar(dist_c[:, :, :], dist_c[:, :, :], CLEN - 1 - (CLEN - 1) / 2.0, None, ALU.add).then_inc(masks, 1)
            g.affine_select(out=row_mask[:, 0:1], in_=row_mask[:, 0:1], compare_op=ALU.is_ge, fill=0.0,
                            base=-(CLEN - 1), pattern=[[0, 1]], channel_multiplier=1).then_inc(masks, 1)
            pool.wait_ge(masks, 10 + 2 * HEADS)
            for t in range(TT):
                g.affine_select(out=dist_c[:, t, :], in_=dist_c[:, t, :], compare_op=ALU.is_ge, fill=FILL,
                                base=P * t - (CLEN - 1), pattern=[[-CSTR, NC]], channel_multiplier=1).then_inc(masks, 1)

            pool.wait_ge(scored, 2 * IH)
            g.affine_select(out=work[:, 0:P], in_=score[:, 0:P], compare_op=ALU.is_ge, fill=NEG, base=0,
                            pattern=[[-1, P]], channel_multiplier=1).then_inc(masked, 1)
            g.affine_select(out=work[:, P:], in_=score[:, P:], compare_op=ALU.is_ge, fill=NEG, base=P,
                            pattern=[[-1, T]], channel_multiplier=1).then_inc(masked, 1)

            g_view = [[kvT[:, a, b, :].rearrange("p (n l) -> p l n", l=CSTR) for b in range(GROUPS)] for a in range(2)]
            pool.wait_ge(drained[BO], 2)
            g.memset(x_hl[:, 2 * CLEN * 2 * NB:].bitcast(F32), 0.0).then_inc(x_pad, 1)
            for kv in range(2):
                pool.wait_ge(drained[BT], T_KC + kv)
                for grp in range(GROUPS):
                    for half in range(CLEN // CSTR):
                        l0 = half * CSTR
                        pe0 = (V_PEK, V_PEV)[kv] + l0
                        g.tensor_tensor(xf[:, kv, l0:l0 + CSTR, grp * NC:(grp + 1) * NC],
                                        g_view[kv][grp][:, :, half:half + NC],
                                        vecT[:, pe0:pe0 + CSTR].unsqueeze(2).to_broadcast([P, CSTR, NC]),
                                        ALU.add).then_inc(xf_ready, 1)

            def k_power(n):
                pool.wait_ge(ss_k, 4 * (n + 1))
                g.tensor_scalar(rk[:, n, :], ssk[:, n, :], 1.0 / DH, EPS, ALU.mult, ALU.add).then_inc(rk_step, 1)
                pool.wait_ge(rk_step, n + 1)
                g.tensor_tensor(rk[:, n, :], rk[:, n, :], m_half[:, 0:4], ALU.pow).then_inc(rk_ready, 1)

            k_power(0)
            k_power(1)
            pool.wait_ge(ss_c, 1)
            g.tensor_scalar(rc[:, :], ssc[:, :], 1.0 / DH, EPS, ALU.mult, ALU.add).then_inc(ss_c, 1)
            pool.wait_ge(ss_c, 2)
            g.tensor_tensor(rc[:, :], rc[:, :], m_half[0:NB, 0:1], ALU.pow).then_inc(ss_c, 1)
            k_power(2)

            def q_power(i):
                pool.wait_ge(ss_q, i * 4 + 4)
                g.tensor_tensor(rq[:, :], ssq[:, :], q_eps[:, :], ALU.add).then_inc(rq_step, 1)
                pool.wait_ge(rq_step, i * 2 + 1)
                g.tensor_tensor(rq[:, :], rq[:, :], m_half[:, 0:4], ALU.pow).then_inc(rq_step, 1)
                pool.wait_ge(rq_step, i * 2 + 2)
                s = inv_slopes[:, bass.ds(i, 1), :].rearrange("p a b -> p (a b)")
                g.tensor_tensor(rq[:, :], rq[:, :], s, ALU.mult).then_inc(rq_ready, 1)

            with pool.Fori(0, HEADS) as i:
                q_power(i)

            pool.wait_ge(x2_ss, 8)
            g.tensor_tensor(ssp[:, :, 0:2], ssp[:, :, 0:2], ssp[:, :, 2:4], ALU.add).then_inc(ss2_step, 1)
            pool.wait_ge(ss2_step, 1)
            g.tensor_tensor(ssp2[:, :], ssp[:, :, 0], ssp[:, :, 1], ALU.add).then_inc(ss2_step, 1)
            pool.wait_ge(ss2_step, 2)
            g.tensor_scalar(ssp2[:, :], ssp2[:, :], 1.0 / D, EPS, ALU.mult, ALU.add).then_inc(ss2_step, 1)
            pool.wait_ge(ss2_step, 3)
            g.tensor_tensor(ssp2[:, :], ssp2[:, :], m_half[:, 0:TT], ALU.pow).then_inc(ss2_step, 1)
            pool.wait_ge(ss2_step, 4)
            g.tensor_scalar(half_rstd[:, :], ssp2[:, :], 0.5, None, ALU.mult).then_inc(r2_ready, 1)

        @block.scalar
        def _(act):
            s = nc.scalar
            act.wait_ge(consts, 2)
            s.activation(warm[:, :], m_half[:, 0:1], ACT.Tanh)
            def rounded(k0, i=0, per=0):
                if k0 == 0:
                    act.wait_ge(piece0_in, 16)
                else:
                    wait_landed(act, k0 // 2, i, per // 2)
                if k0 >= RING:
                    act.wait_ge(piece_used, i * per + k0 - RING + 1)
                n = 8 * N_SMALL if P_A0 <= k0 < P_A2 else 1024
                s.activation(w_hi[:, k0 % RING, 0:n], raw[:, (k0 // 2) % RAW, k0 % 2, 0:n], ACT.Copy).then_inc(hi_ready, 1)

            def copied(b, n, dst, src, scale=1.0):
                act.wait_ge(filled[b], n)
                s.activation(dst, src, ACT.Copy, scale=scale).then_inc(drained[b], 1)

            def evacuated(b, end, parts, scale=None):
                if end:
                    act.wait_ge(piece_used, end)
                for t, dst, lo, hi in parts:
                    src = acc[b][t][:, lo:hi]
                    if len(dst.shape) == 3:
                        src = src.rearrange("p (g d) -> p g d", g=GROUPS)
                    e = s.activation(dst, src, ACT.Copy, scale=scale or rstd[:, t:t + 1])
                e.then_inc(acc_out[b], 1)

            def hT_upper(u):
                b, n = X_BANKS[u % 4], X_USES[u % 4] + u // 4
                act.wait_ge(filled[b], n)
                for kt in (2 * u, 2 * u + 1):
                    s.activation(hT_hi[:, kt, :], aux[b][:, (kt % 2) * T:(kt % 2 + 1) * T], ACT.Copy,
                                 scale=normT[:, kt:kt + 1]).then_inc(t_hi, 1)

            def index_head(hh):
                b = BS0 + hh % 2
                act.wait_ge(filled[b], S_IDX + hh // 2)
                if hh >= 2:
                    act.wait_ge(scored, 2 * (hh - 1))
                s.activation(rel[:, hh % 2, :], aux[b][:, 0:3 * P], ACT.Relu).then_inc(drained[b], 1)

            def hidden_out(kv):
                act.wait_ge(piece_used, P_MIX + 16 * kv + 14)
                s.activation(th[0:2 * NB, 1, TH_HID:TH_HID + HID], aux[BS0 + kv][0:2 * NB, 0:HID], ACT.Copy).then_inc(hid_out, 1)

            def hidden(kv):
                b = BS0 + kv
                act.wait_ge(filled[b], S_W1)
                s.activation(hz[:, kv, :], aux[b][0:NB, HID:2 * HID], ACT.Copy)
                s.activation(hth[:, kv, :], aux[b][0:NB, HID:2 * HID], ACT.Tanh, scale=0.5).then_inc(drained[b], 1)

            copied(BT, T_NORM, normT[:, :], aux[BT][:, 0:KD])
            act.wait_ge(drained[BT], T_NORM)
            for k in range(AHEAD):
                hT_upper(k)
                rounded(k)
            for k in range(P_L):
                rounded(k + AHEAD)
                if k + AHEAD < KD // 2:
                    hT_upper(k + AHEAD)
                if k == 3:
                    for part_in in x_in:
                        act.wait_ge(part_in, 16)
                    s.activation(th[:, 0, D:2 * D], x_nat[:, 0, :], ACT.Square, accum_out=ssx[:, 0:1]).then_inc(ss_x, 1)
                if k == P_A0:
                    act.wait_ge(filled[BT], T_PLE)
                    s.activation(pT_hi[:, :, :], aux[BT][:, :].rearrange("p (k t) -> p k t", k=2), ACT.Copy).then_inc(p_hi, 1)
                if k == P_A2:
                    act.wait_ge(piece_used, P_A2)
                    s.activation(th[0:N_SMALL, 0, TH_SMALL:TH_SMALL + T], acc[1][0][0:N_SMALL, 0:T], ACT.Copy).then_inc(acc_out[1], 1)
                if k == P_A2 + 2:
                    act.wait_ge(filled[BT], T_SMALL)
                    for t in range(TT):
                        at = t * N_SMALL
                        s.activation(th[:, t, TH_NG:TH_NG + N_SMALL], aux[BT][:, at:at + N_SMALL], ACT.Copy, scale=rstd[:, t:t + 1])
                        for d in range(2):
                            e = s.activation(th[:, t, TH_IK2 + d * ID:TH_IK2 + (d + 1) * ID], aux[BT][:, at + 24:at + 24 + ID],
                                             ACT.Copy, scale=rstd[:, t:t + 1])
                    e.then_inc(drained[BT], 1)
                if k == P_A2 + 3:
                    act.wait_ge(drained[BT], T_SMALL)
                    s.activation(tmp24[:, :, :], th[:, :, TH_NG:TH_NG + 24], ACT.Tanh, scale=0.5).then_inc(ng_tanh, 1)
                if k == P_A2 + 4:
                    copied(BT, T_IK, ikT[:, :], aux[BT][:, 0:T])
                if k == P_A0:
                    act.wait_ge(rstd_ready, 3)
                    evacuated(0, P_A0, [(t, th[:, t, 0:NCOL], 0, NCOL) for t in range(TT)])
                for u, at in enumerate((15, 16, 20, 21)):
                    if k == at:
                        copied(BT, T_IQ + u, iqT[:, 2 * u:2 * u + 2, :], aux[BT][:, :].rearrange("p (k t) -> p k t", k=2))
                for hh in range(0, IH, 2):
                    if k == (17 + hh // 2 if hh < 8 else 19 + hh // 2):
                        index_head(hh)
                        index_head(hh + 1)
                if k == P_A2 + 8:
                    evacuated(0, P_A3, [(t, th[:, t, NCOL:2 * NCOL], 0, NCOL) for t in range(TT)])
                if k == P_A3 + 8:
                    evacuated(1, P_A4, [(t, th[:, t, TH_KC:TH_KC + NCOL], 0, NCOL) for t in range(TT)])
                for kv in range(2):
                    if k == 28 + kv:
                        act.wait_ge(filled[BT], T_KC + kv)
                        s.activation(kvT[:, kv, :, :], aux[BT][:, :].rearrange("p (g t) -> p g t", g=GROUPS),
                                     ACT.Copy).then_inc(drained[BT], 1)
                    if k == 31 + kv:
                        act.wait_ge(xf_ready, 4 * (kv + 1))
                        s.activation(x_split[:, kv, :, 0, :], xf[:, kv, :, :], ACT.Copy).then_inc(x_hi_ready, 1)
                for b, at, br, col in ((0, P_A4 + 8, 0, TH_KS), (1, P_MIX + 16, 1, TH_KW), (0, P_Q0, 2, TH_DK)):
                    if k == at:
                        evacuated(b, at, [(t, th[:, t, col:col + 256], 0, 256) for t in range(TT)]
                                  + [(t, v_all[:, br, t, :, :], 256, 512) for t in range(TT)])
                for br, at, n in ((0, 47, T_KS), (1, 54, T_KW), (2, 70, T_DK)):
                    if k == at:
                        copied(BT, n, kT[:, br, :, :], aux[BT][:, :].rearrange("p (g t) -> p g t", g=GROUPS),
                               scale=k_gain[:, br + 1:br + 2])
                for kv, n in ((0, T_HK), (1, T_HV)):
                    if k == 48 + 16 * kv:
                        hidden_out(kv)
                    if k == 50 + 16 * kv:
                        hidden(kv)
                    if k == (53, 69)[kv]:
                        copied(BT, n, hidT[:, 2 * kv:2 * kv + 2, :], aux[BT][:, 0:2 * NB].rearrange("p (a n) -> p a n", a=2))
                if k == 55:
                    copied(BT, T_KC2, kc_nat[:, :], aux[BT][0:NB, 0:DH], scale=0.5)
                if k == 71:
                    copied(BT, T_VC2, vc[:, :, :], aux[BT][0:NC, 0:2 * DH].rearrange("p (g d) -> p g d", g=GROUPS), scale=0.5)
                if k == 59:
                    copied(BT, T_KCN, kcT[:, :], aux[BT][:, 0:NB], scale=k_gain[:, 0:1])

            def qz_out(n):
                act.wait_ge(piece_used, n * 16 + P_L)
                for t in range(TT):
                    s.activation(q_raw[:, t, :, :, :], acc[1][t][:, :].rearrange("p (m s d) -> p m s d", m=2, s=2), ACT.Copy,
                                 scale=rstd[:, t:t + 1]).then_inc(q_out if t == 0 else acc_out[1], 1)
                act.wait_ge(q_out, n + 1)
                act.wait_ge(acc_out[1], n + ACC_L)
                s.activation(z_gate[:, :, :, :], q_raw[:, :, :, 1, :], ACT.Tanh, scale=0.5).then_inc(z_tanh, 1)

            def attend(k, i):
                if k == 3:
                    copied(BT, i * 5 + T_L, qT[:, :, :], aux[BT][:, :].rearrange("p (m t) -> p m t", m=2))
                if k == 4:
                    act.wait_ge(neg_ready, i * 2 + 1)
                    for t in range(TT):
                        s.activation(prob[:, 0, t * P:(2 * t + 1) * P], prob[:, 0, t * P:(2 * t + 1) * P], ACT.Exp,
                                     bias=neg_mx[:, 2 + t:3 + t], accum_out=rowsum[:, t, 1:2])
                    for t in range(TT):
                        e = s.activation(prob_c[:, t, :], prob_c[:, t, :], ACT.Exp, bias=neg_mx[:, t:t + 1],
                                         accum_out=rowsum[:, t, 0:1])
                    e.then_inc(exp_ready, 1)
                    for t in range(TT):
                        e = s.activation(prob[:, 1, t * P:(2 * t + 1) * P], prob[:, 1, t * P:(2 * t + 1) * P], ACT.Exp,
                                         bias=neg_mx[:, 4 + t:5 + t], accum_out=rowsum[:, t, 2:3])
                    e.then_inc(exp_ready, 1)
                if k == 5:
                    act.wait_ge(neg_ready, i * 2 + 2)
                    for t in range(TT):
                        e = s.activation(prob[:, 2, t * P:(2 * t + 1) * P], prob[:, 2, t * P:(2 * t + 1) * P], ACT.Exp,
                                         bias=neg_mx[:, 6 + t:7 + t], accum_out=rowsum[:, t, 3:4])
                    e.then_inc(exp_ready, 1)
                if k == 6:
                    copied(BT, i * 5 + T_L + 1, probT[:, 0, :], aux[BT][:, 0:3 * P])
                    copied(BO, i * 2 + O_L, prob_cT[:, :], aux[BO][0:NC, 0:T])
                if k == 7:
                    copied(BT, i * 5 + T_L + 2, probT[:, 1, :], aux[BT][:, 0:3 * P])
                if k == 8:
                    copied(BT, i * 5 + T_L + 3, probT[:, 2, :], aux[BT][:, 0:3 * P])
                if k == 8:
                    act.wait_ge(piece_used, i * 16 + P_L + 8)
                    for t in range(TT):
                        e = s.activation(th[:, t, bass.ds(i * NCOL, NCOL)], acc[0][t][:, :], ACT.Tanh, scale=half_rstd_x[:, t:t + 1])
                    e.then_inc(acc_out[0], 1)
                if k == 11:
                    act.wait_ge(filled[BT], i * 5 + T_L + 4)
                    s.activation(oT_hi[:, :, :].rearrange("p (m h) t -> p m h t", m=2)[:, :, bass.ds(i, 1), :].rearrange("p m h t -> p m (h t)"),
                                 aux[BT][:, :].rearrange("p (m t) -> p m t", m=2), ACT.Copy).then_inc(o_hi, 1)

            qz_out(0)
            with act.Fori(0, HEADS - 1) as i:
                for k in range(16):
                    rounded(P_L + k + AHEAD, i, 16)
                    attend(k, i)
                qz_out(i + 1)
            for k in range(8):
                rounded(P_L7 + k + AHEAD)
                attend(k, HEADS - 1)

            def yT_upper(j):
                for b, n in ((BT, T_Y), (BO, O_Y)):
                    act.wait_ge(filled[b], j + n)
                    s.activation(hT_hi[:, bass.ds(j * 4 + (0 if b == BT else 2), 2), :],
                                 aux[b][:, :].rearrange("p (k t) -> p k t", k=2), ACT.Copy).then_inc(y_hi, 1)

            def up_block(j, first):
                for k in range(8):
                    rounded(P_U + k + AHEAD, j, 8)
                    if k == 2 and not first:
                        yT_upper(j - 1)
                    if first:
                        attend(8 + k, HEADS - 1)

            up_block(0, True)
            with act.Fori(1, 4) as j:
                up_block(j, False)

            def embedded(q):
                col = D + q * NCOL
                if q % 2 == 0:
                    act.wait_ge(ple_made, q // 2 + 1)
                evacuated(1 - q % 2, P_PP + q + 1 if q % 2 else 0, [(t, th[:, t, col:col + NCOL], 0, NCOL) for t in range(TT)], scale=0.5)

            for k in range(4):
                rounded(P_PP + k + AHEAD)
                if k:
                    embedded(k - 1)
                if k == 2:
                    yT_upper(3)

            def x2T_upper(j):
                for b, n in ((BT, T_X), (BO, O_X)):
                    act.wait_ge(filled[b], n + j)
                    for q in range(2):
                        kt = 4 * j + q + (0 if b == BT else 2)
                        s.activation(oT_hi[:, kt, :], aux[b][:, q * T:(q + 1) * T], ACT.Copy,
                                     scale=vecT[:, V_PLE + kt:V_PLE + kt + 1]).then_inc(x2_hi, 1)

            for j in range(4):
                for k in range(8):
                    rounded(P_O + 8 * j + k + AHEAD)
                    if j == 0 and k == 0:
                        embedded(3)
                    if j and k == 3:
                        x2T_upper(j - 1)

            for j in range(4):
                for k in range(8):
                    if P_G + 8 * j + k + AHEAD < N_PIECES:
                        rounded(P_G + 8 * j + k + AHEAD)
                    if j == 0 and k == 3:
                        x2T_upper(3)
                b = (j + 1) % 2
                act.wait_ge(r2_ready, 1)
                for t in range(TT):
                    if j == 3 and t == 0:
                        act.wait_ge(first_tile_done, 1)
                    else:
                        act.wait_ge(piece_used, P_G + 8 * j + 8)
                    if j:
                        act.wait_ge(out_ready, 2 * j - 1 + t)
                    s.activation(stage[:, t, :], acc[b][t][:, :], ACT.Tanh, scale=half_rstd[:, t:t + 1]).then_inc(g_tanh, 1)

        @block.vector
        def _(dve):
            v = nc.vector

            def rest(k0, i=0, per=0):
                dve.wait_ge(hi_ready, i * per + k0 + 1)
                n = 8 * N_SMALL if P_A0 <= k0 < P_A2 else 1024
                v.tensor_tensor(w_lo[:, k0 % RING, 0:n], raw[:, (k0 // 2) % RAW, k0 % 2, 0:n],
                                w_hi[:, k0 % RING, 0:n].bitcast(F32), ALU.subtract).then_inc(lo_ready, 1)



            def hT_rest(u):
                b = X_BANKS[u % 4]
                dve.wait_ge(t_hi, 2 * u + 2)
                for kt in (2 * u, 2 * u + 1):
                    e = v.scalar_tensor_tensor(out=hT_lo[:, kt, :], in0=aux[b][:, (kt % 2) * T:(kt % 2 + 1) * T],
                                               scalar=normT[:, kt:kt + 1],
                                               in1=hT_hi[:, kt, :].bitcast(F32), op0=ALU.mult, op1=ALU.subtract)
                e.then_inc(drained[b], 1)

            def index_sum(hh):
                b = BS0 + hh % 2
                dve.wait_ge(drained[b], S_IDX + hh // 2)
                for t in range(TT):
                    part = slice(t * P, (2 * t + 1) * P)
                    w = th[:, t, TH_IW + hh:TH_IW + hh + 1]
                    if hh == 0:
                        v.tensor_scalar(score[:, part], rel[:, 0, part], w, None, ALU.mult).then_inc(scored, 1)
                    else:
                        dve.wait_ge(scored, 2 * hh - 1 + t)
                        v.scalar_tensor_tensor(out=score[:, part], in0=rel[:, hh % 2, part], scalar=w,
                                               in1=score[:, part], op0=ALU.mult, op1=ALU.add).then_inc(scored, 1)

            def topk_round(r):
                if r == 0:
                    dve.wait_ge(masked, 2)
                for t in range(TT):
                    part = slice(t * P, (2 * t + 1) * P)
                    if r:
                        dve.wait_ge(topk_step, 4 * r - 1 + t)
                    v.max(top8[:, t, :], work[:, part]).then_inc(topk_step, 1)
                for t in range(TT):
                    part = slice(t * P, (2 * t + 1) * P)
                    dve.wait_ge(topk_step, 4 * r + 1 + t)
                    v.match_replace(work[:, part], top8[:, t, :], work[:, part], TAKEN).then_inc(topk_step, 1)

            def k_squares(br, col):
                for t in range(TT):
                    for grp in range(GROUPS):
                        kk = th[:, t, col + grp * DH:col + (grp + 1) * DH]
                        v.tensor_tensor_reduce(th[:, t, 3328 + grp * DH:3328 + (grp + 1) * DH], kk, kk, 1.0, 0.0, ALU.mult,
                                               ALU.add, ssk[:, br, 2 * t + grp:2 * t + grp + 1]).then_inc(ss_k, 1)

            def k_normed(br, col):
                dve.wait_ge(rk_ready, br + 1)
                for t in range(TT):
                    for grp in range(GROUPS):
                        kk = th[:, t, col + grp * DH:col + (grp + 1) * DH]
                        v.tensor_scalar(kk, kk, rk[:, br, 2 * t + grp:2 * t + grp + 1], None, ALU.mult).then_inc(kn_ready, 1)

            for k in range(AHEAD):
                hT_rest(k)
                rest(k)
            for k in range(P_L):
                rest(k + AHEAD)
                if k + AHEAD < KD // 2:
                    hT_rest(k + AHEAD)
                if k == 3:
                    for part_in in x_in:
                        dve.wait_ge(part_in, 16)
                    v.tensor_tensor_reduce(th[:, 1, D:2 * D], x_nat[:, 1, :], x_nat[:, 1, :], 1.0, 0.0, ALU.mult, ALU.add,
                                           ssx[:, 1:2]).then_inc(ss_x, 1)
                if k == P_A0:
                    dve.wait_ge(p_hi, 1)
                    v.tensor_tensor(pT_lo[:, :, :], aux[BT][:, :].rearrange("p (k t) -> p k t", k=2),
                                    pT_hi[:, :, :].bitcast(F32), ALU.subtract).then_inc(drained[BT], 1)
                if k == P_A0 + 1:
                    dve.wait_ge(filled[BT], T_VEC)
                    v.tensor_copy(vecT[:, :], aux[BT][:, 0:N_VEC]).then_inc(drained[BT], 1)
                    dve.wait_ge(drained[BT], T_VEC)
                    v.tensor_scalar(k_gain[:, 0:3], vecT[:, V_KC:V_KC + 3], vecT[:, V_NQ:V_NQ + 1], None, ALU.mult).then_inc(gain_ready, 1)
                    v.tensor_tensor(k_gain[:, 3:4], vecT[:, V_DQ:V_DQ + 1], vecT[:, V_DK:V_DK + 1], ALU.mult).then_inc(gain_ready, 1)
                if k == P_A2 + 4:
                    dve.wait_ge(ng_tanh, 1)
                    dve.wait_ge(masks, 12 + 2 * HEADS)
                    for t in range(TT):
                        v.tensor_scalar(gates[:, t, :, 0:3], tmp24[:, t, :].rearrange("p (h b) -> p h b", b=3), 0.25, 0.25,
                                        ALU.mult, ALU.add).then_inc(gates_step, 1)
                    for t in range(TT):
                        dve.wait_ge(gates_step, t + 1)
                        v.tensor_scalar(gates[:, t, :, 0], gates[:, t, :, 0], row_mask[:, t:t + 1], None,
                                        ALU.mult).then_inc(gates_ready, 1)
                for hh in range(0, IH, 2):
                    if k == (18 + hh // 2 if hh < 8 else 20 + hh // 2):
                        index_sum(hh)
                        index_sum(hh + 1)
                if k in TOPK_AT:
                    topk_round(TOPK_AT.index(k))
                if k == 41:
                    dve.wait_ge(topk_step, 4 * (TOPK // 8))
                    v.tensor_scalar(dist_dsa[:, :], work[:, :], 0.5 * TAKEN, FILL, ALU.is_gt, ALU.mult).then_inc(dsa_ready, 1)
                    dve.wait_ge(dsa_ready, 1)
                    v.tensor_tensor(dist_dsa[:, :], dist_dsa[:, :], dist[:, :], ALU.add).then_inc(dsa_ready, 1)
                for kv in range(2):
                    if k == 32 + kv:
                        dve.wait_ge(x_hi_ready, kv + 1)
                        v.tensor_tensor(x_split[:, kv, :, 1, :], xf[:, kv, :, :], x_split[:, kv, :, 0, :].bitcast(F32),
                                        ALU.subtract).then_inc(x_lo_ready, 1)
                    if k == 51 + 16 * kv:
                        dve.wait_ge(drained[BS0 + kv], S_W1)
                        v.scalar_tensor_tensor(out=hth[:, kv, :], in0=hth[:, kv, :], scalar=1.0, in1=hz[:, kv, :],
                                               op0=ALU.add, op1=ALU.mult).then_inc(hid_ready, 1)
                for br, at, b, n, col in ((0, 44, 0, 3, TH_KS), (1, 51, 1, 3, TH_KW), (2, 67, 0, 4, TH_DK)):
                    if k == at:
                        dve.wait_ge(acc_out[b], n)
                        if br:
                            dve.wait_ge(ss_k, 4 * br)
                        k_squares(br, col)
                    if k == at + 1:
                        k_normed(br, col)
                if k == 56:
                    dve.wait_ge(drained[BT], T_KC2)
                    v.tensor_tensor_reduce(kc_junk[:, :], kc_nat[:, :], kc_nat[:, :], 1.0, 0.0, ALU.mult, ALU.add,
                                           ssc[:, :]).then_inc(ss_c, 1)
                if k == 57:
                    dve.wait_ge(ss_c, 3)
                    v.tensor_scalar(kc_nat[:, :], kc_nat[:, :], rc[:, :], None, ALU.mult).then_inc(kcn_ready, 1)

            def fence(n):
                v.memset(fence_col[:, n:n + 1], 0.0)

            def scores(src, dist_ap, dst, m):
                return v.tensor_tensor_reduce(dst, src, dist_ap, slope[:, 0:1], -3e38, ALU.add, ALU.max, mx[:, m:m + 1])

            def attend(k, i):
                if k == 0:
                    dve.wait_ge(acc_out[1], i + ACC_L)
                    dve.wait_ge(q_out, i + 1)
                    v.tensor_copy(slope[:, :], slopes[:, bass.ds(i, 1)]).then_inc(slope_ready, 1)
                    for t in range(TT):
                        for m in range(2):
                            qq = q_raw[:, t, m, 0, :]
                            v.tensor_tensor_reduce(q_n[:, t, m, :], qq, qq, 1.0, 0.0, ALU.mult, ALU.add,
                                                   ssq[:, 2 * t + m:2 * t + m + 1]).then_inc(ss_q, 1)
                if k == 1:
                    dve.wait_ge(rq_ready, i + 1)
                    for t in range(TT):
                        for m in range(2):
                            e = v.tensor_scalar(q_n[:, t, m, :], q_raw[:, t, m, 0, :], rq[:, 2 * t + m:2 * t + m + 1], None,
                                                ALU.mult)
                    e.then_inc(qn_ready, 1)
                if k == 2:
                    dve.wait_ge(z_tanh, i + 1)
                    for t in range(TT):
                        e = v.scalar_tensor_tensor(out=z_gate[:, t, :, :], in0=z_gate[:, t, :, :], scalar=1.0,
                                                   in1=q_raw[:, t, :, 1, :], op0=ALU.add, op1=ALU.mult)
                    e.then_inc(z_ready, 1)
                if k == 4:
                    dve.wait_ge(slope_ready, i + 1)
                    dve.wait_ge(filled[BS0], i * 2 + S_L)
                    fence(0)
                    for t in range(TT):
                        part = slice(t * P, (2 * t + 1) * P)
                        scores(aux[BS0][:, part], dist[:, part], prob[:, 0, part], 2 + t)
                    for t in range(TT):
                        e = scores(aux[BS0][:, 3 * P + t * 16:3 * P + t * 16 + NC], dist_c[:, t, :], prob_c[:, t, :], t)
                    e.then_inc(drained[BS0], 1)
                    dve.wait_ge(filled[BS1], i * 2 + S_L)
                    fence(1)
                    for t in range(TT):
                        part = slice(t * P, (2 * t + 1) * P)
                        e = scores(aux[BS1][:, part], dist[:, part], prob[:, 1, part], 4 + t)
                    e.then_inc(drained[BS1], 1)
                    dve.wait_ge(drained[BS1], i * 2 + S_L)
                    v.tensor_scalar(neg_mx[:, 0:6], mx[:, 0:6], -1.0, None, ALU.mult).then_inc(neg_ready, 1)
                if k == 5:
                    dve.wait_ge(filled[BS0], i * 2 + S_L + 1)
                    fence(2)
                    for t in range(TT):
                        part = slice(t * P, (2 * t + 1) * P)
                        e = scores(aux[BS0][:, part], dist_dsa[:, part], prob[:, 2, part], 6 + t)
                    e.then_inc(drained[BS0], 1)
                    dve.wait_ge(drained[BS0], i * 2 + S_L + 1)
                    v.tensor_scalar(neg_mx[:, 6:8], mx[:, 6:8], -1.0, None, ALU.mult).then_inc(neg_ready, 1)
                if k == 7:
                    dve.wait_ge(exp_ready, i * 3 + 3)
                    v.reciprocal(rrow[:, :, :], rowsum[:, :, :]).then_inc(coef_step, 1)
                    dve.wait_ge(coef_step, i + 1)
                    v.tensor_tensor(coef[:, :, :], rrow[:, :, :],
                                    gates[:, :, bass.ds(i, 1), :].rearrange("p t h b -> p t (h b)"), ALU.mult).then_inc(coef_ready, 1)
                    dve.wait_ge(coef_ready, i + 1)
                    dve.wait_ge(filled[BO], i * 2 + O_L + 1)
                    for t in range(TT):
                        v.tensor_scalar(o_nat[:, 0, t, :], aux[BO][:, t * P:(t + 1) * P], coef[:, t, 0:1], None,
                                        ALU.mult).then_inc(o_step, 1)
                    for t in range(TT):
                        dve.wait_ge(o_step, i * 2 + 1 + t)
                        e = v.scalar_tensor_tensor(out=o_nat[:, 0, t, :], in0=aux[BO][:, T + t * P:T + (t + 1) * P],
                                                   scalar=coef[:, t, 1:2], in1=o_nat[:, 0, t, :], op0=ALU.mult, op1=ALU.add)
                    e.then_inc(drained[BO], 1)
                if k == 9:
                    dve.wait_ge(filled[BS1], i * 2 + S_L + 1)
                    dve.wait_ge(z_ready, i + 1)
                    dve.wait_ge(drained[BO], i * 2 + O_L + 1)
                    for t in range(TT):
                        v.scalar_tensor_tensor(out=o_nat[:, 0, t, :], in0=aux[BS1][:, t * P:(t + 1) * P],
                                               scalar=coef[:, t, 2:3], in1=o_nat[:, 0, t, :], op0=ALU.mult, op1=ALU.add)
                    for t in range(TT):
                        e = v.scalar_tensor_tensor(out=o_nat[:, 1, t, :], in0=aux[BS1][:, T + t * P:T + (t + 1) * P],
                                                   scalar=coef[:, t, 3:4], in1=z_gate[:, t, 1, :], op0=ALU.mult,
                                                   op1=ALU.mult)
                    e.then_inc(drained[BS1], 1)
                    dve.wait_ge(drained[BS1], i * 2 + S_L + 1)
                    v.tensor_tensor(o_nat[:, 0, :, :], o_nat[:, 0, :, :], z_gate[:, :, 0, :], ALU.mult).then_inc(o_ready, 1)
                if k == 11:
                    dve.wait_ge(o_hi, i + 1)
                    head = [a[:, :, :].rearrange("p (m h) t -> p m h t", m=2)[:, :, bass.ds(i, 1), :].rearrange("p m h t -> p m (h t)")
                            for a in (oT_hi, oT_lo)]
                    e = v.tensor_tensor(head[1], aux[BT][:, :].rearrange("p (m t) -> p m t", m=2), head[0].bitcast(F32), ALU.subtract)
                    e.then_inc(drained[BT], 1)

            with dve.Fori(0, HEADS - 1) as i:
                for k in range(16):
                    rest(P_L + k + AHEAD, i, 16)
                    attend(k, i)
            for k in range(8):
                rest(P_L7 + k + AHEAD)
                attend(k, HEADS - 1)

            def yT_rest(j):
                for b, n, o in ((BT, 1, 0), (BO, 2, 2)):
                    dve.wait_ge(y_hi, j * 2 + n)
                    e = v.tensor_tensor(hT_lo[:, bass.ds(j * 4 + o, 2), :], aux[b][:, :].rearrange("p (k t) -> p k t", k=2),
                                        hT_hi[:, bass.ds(j * 4 + o, 2), :].bitcast(F32), ALU.subtract)
                    e.then_inc(drained[b], 1)

            def up_block(j, first):
                for k in range(8):
                    rest(P_U + k + AHEAD, j, 8)
                    if k == 2 and not first:
                        yT_rest(j - 1)
                    if first:
                        attend(8 + k, HEADS - 1)
                    if k == 6:
                        dve.wait_ge(piece_used, j * 8 + P_U + 6)
                        for t in range(TT):
                            g = th[:, t, bass.ds(j * NCOL, NCOL)]
                            e = v.scalar_tensor_tensor(out=g, in0=g, scalar=1.0, in1=acc[1][t][:, :], op0=ALU.add, op1=ALU.mult)
                        e.then_inc(acc_out[1], 1)
                dve.wait_ge(piece_used, j * 8 + P_U + 8)
                for t in range(TT):
                    g = th[:, t, bass.ds(j * NCOL + D, NCOL)]
                    e = v.scalar_tensor_tensor(out=g, in0=g, scalar=1.0, in1=acc[0][t][:, :], op0=ALU.add, op1=ALU.mult)
                e.then_inc(acc_out[0], 1)
                dve.wait_ge(acc_out[1], j + ACC_L + 8)
                dve.wait_ge(acc_out[0], j + ACC_L + 9)
                for t in range(TT):
                    e = v.tensor_tensor(stage[:, t, :], th[:, t, bass.ds(j * NCOL, NCOL)], th[:, t, bass.ds(j * NCOL + D, NCOL)],
                                        ALU.add)
                e.then_inc(y_ready, 1)

            up_block(0, True)
            with dve.Fori(1, 4) as j:
                up_block(j, False)
            for k in range(4):
                rest(P_PP + k + AHEAD)
                if k == 2:
                    yT_rest(3)

            def x2T_rest(j):
                for b, o in ((BT, 0), (BO, 2)):
                    dve.wait_ge(x2_hi, 4 * j + o + 2)
                    for q in range(2):
                        kt = 4 * j + o + q
                        e = v.scalar_tensor_tensor(out=oT_lo[:, kt, :], in0=aux[b][:, q * T:(q + 1) * T],
                                                   scalar=vecT[:, V_PLE + kt:V_PLE + kt + 1],
                                                   in1=oT_hi[:, kt, :].bitcast(F32), op0=ALU.mult, op1=ALU.subtract)
                    e.then_inc(drained[b], 1)

            for j in range(4):
                for k in range(8):
                    rest(P_O + 8 * j + k + AHEAD)
                    if j and k == 3:
                        x2T_rest(j - 1)
                b, n = (j + 1) % 2, ACC_L + (14, 15, 15, 16)[j]
                dve.wait_ge(piece_used, P_O + 8 * j + 8)
                if j == 0:
                    dve.wait_ge(xr_in, 32)
                for t in range(TT):
                    part = xr[:, t, j * NCOL:(j + 1) * NCOL]
                    e = v.scalar_tensor_tensor(out=part, in0=acc[b][t][:, :], scalar=0.5, in1=part, op0=ALU.mult, op1=ALU.add)
                e.then_inc(acc_out[b], 1)
                dve.wait_ge(acc_out[b], n)
                for t in range(TT):
                    part = xr[:, t, j * NCOL:(j + 1) * NCOL]
                    if j:
                        dve.wait_ge(x2_ss, 2 * j - 1 + t)
                    v.tensor_tensor_reduce(th[:, t, 0:NCOL], part, part, 1.0, 0.0, ALU.mult, ALU.add,
                                           ssp[:, t, j:j + 1]).then_inc(x2_ss, 1)

            for j in range(4):
                for k in range(8):
                    if P_G + 8 * j + k + AHEAD < N_PIECES:
                        rest(P_G + 8 * j + k + AHEAD)
                    if j == 0 and k == 3:
                        x2T_rest(3)
                for t in range(TT):
                    dve.wait_ge(g_tanh, 2 * j + t + 1)
                    v.scalar_tensor_tensor(out=stage[:, t, :], in0=stage[:, t, :], scalar=1.0,
                                           in1=th[:, t, D + j * NCOL:D + (j + 1) * NCOL], op0=ALU.add, op1=ALU.mult
                                           ).then_inc(gated, 1)
                    dve.wait_ge(gated, 2 * j + t + 1)
                    part = xr[:, t, j * NCOL:(j + 1) * NCOL]
                    v.tensor_tensor(part, part, stage[:, t, :], ALU.add).then_inc(out_ready, 1)

        @block.tensor
        def _(pe):
            m = nc.tensor

            def bank_free(b, n):
                if isinstance(n, int) and n <= 1:
                    return
                pe.wait_ge(drained[b], n - 1)

            def piece(k0, kts, hi, lo, b, first, last, width=NCOL, cols=NCOL, i=0, per=0, at=None, tiles=range(TT)):
                pe.wait_ge(lo_ready, i * per + k0 + 1)
                s = k0 % RING
                for q, kt in enumerate(kts):
                    c = (at or 0) + q * width
                    wh, wl = w_hi[:, s, c:c + cols], w_lo[:, s, c:c + cols]
                    for t in tiles:
                        o = acc[b][t][:, 0:cols]
                        st, en = first and q == 0, last and q == len(kts) - 1
                        xh, xl = hi[:, kt, t * P:(t + 1) * P], lo[:, kt, t * P:(t + 1) * P]
                        m.matmul(o, xh, wh, start=st, stop=False)
                        m.matmul(o, xh, wl, start=False, stop=False)
                        e = m.matmul(o, xl, wh, start=False, stop=en)
                if at is not None:
                    return e
                e.then_inc(piece_used, 1)

            def turned(b, n, sources):
                bank_free(b, n)
                at = 0
                for src in sources:
                    rows, w = src.shape[0], src.shape[-1]
                    e = m.transpose(aux[b][0:w, at:at + rows], src, ident[0:rows, 0:rows])
                    at += rows
                e.then_inc(filled[b], 1)

            pe.wait_ge(consts, 4)

            def x_turned(u):
                b, n = X_BANKS[u % 4], X_USES[u % 4] + u // 4
                for c, part_in in enumerate(x_in):
                    if X_PARTS[c] == 2 * u * P:
                        pe.wait_ge(part_in, 16)
                turned(b, n, [x_nat[:, t, kt * P:(kt + 1) * P] for kt in (2 * u, 2 * u + 1) for t in range(TT)])

            def index_head(hh):
                b, part = BS0 + hh % 2, slice((hh % 2) * ID, (hh % 2 + 1) * ID)
                bank_free(b, S_IDX + hh // 2)
                for t in range(TT):
                    e = m.matmul(aux[b][:, t * P:(2 * t + 1) * P], iqT[part, hh // 2, t * P:(t + 1) * P],
                                 ikT[part, 0:(t + 1) * P], start=True, stop=True)
                e.then_inc(filled[b], 1)

            def compress(k, kv, first):
                pe.wait_ge(lo_ready, k + 1)
                s = k % RING
                for q in range(4):
                    l = first + q
                    at = (kv * CLEN + l) * 2 * NB
                    o = aux[BS0 + kv][:, 0:HID]
                    m.matmul(o, x_hl[:, at:at + P], w_hi[:, s, q * HID:(q + 1) * HID], start=(l == 0), stop=False)
                    e = m.matmul(o, x_hl[:, at:at + P], w_lo[:, s, q * HID:(q + 1) * HID], start=False, stop=(l == CLEN - 1))
                e.then_inc(piece_used, 1)

            def small_piece(k):
                pe.wait_ge(lo_ready, k + 1)
                o = acc[1][0][:, 0:T]
                for q in range(8):
                    kt, part = 8 * (k - P_A0) + q, slice(q * N_SMALL, q * N_SMALL + P)
                    wh, wl = w_hi[:, k % RING, part], w_lo[:, k % RING, part]
                    m.matmul(o, wh, hT_hi[:, kt, :], start=(kt == 0), stop=False)
                    m.matmul(o, wh, hT_lo[:, kt, :], start=False, stop=False)
                    e = m.matmul(o, wl, hT_hi[:, kt, :], start=False, stop=(kt == KD - 1))
                e.then_inc(piece_used, 1)

            for _ in range(7):
                m.transpose(aux[BT][:, 0:P], ident[:, :], ident[:, :])
            pe.wait_ge(norm_in, 16)
            turned(BT, T_NORM, [vecs[0:KD, :]])
            x_turned(0)
            for _ in range(6):
                m.transpose(acc[1][0][:, 0:P], ident[:, :], ident[:, :])
            x_turned(1)
            for _ in range(7):
                m.transpose(acc[1][0][:, 0:P], ident[:, :], ident[:, :])
            stages = [(P_A1, 0, 0), (P_A2, 0, 1), (P_A3, 1, 1), (P_A4, 0, 2), (P_Q0, 1, 3)]
            for k in range(P_L):
                if P_A0 <= k < P_A2:
                    small_piece(k)
                elif P_MIX <= k < P_Q0:
                    kv, n = (k - P_MIX) // 16, (k - P_MIX) % 16 // 4 * 2 + k % 2
                    if k == P_MIX:
                        pe.wait_ge(x_lo_ready, 2)
                        pe.wait_ge(x_pad, 1)
                    if (k - P_MIX) % 4 < 2:
                        if n == 0:
                            bank_free(BS0 + kv, S_W1)
                        compress(k, kv, 4 * n)
                    else:
                        if n == 0:
                            pe.wait_ge(acc_out[1 - kv], 2 + kv)
                        piece(k, (2 * n, 2 * n + 1), hT_hi, hT_lo, 1 - kv, n == 0, n == 7)
                else:
                    for at, b, n in stages:
                        if at <= k < at + 8:
                            if k == at and n:
                                pe.wait_ge(acc_out[b], n)
                            if at == P_A1:
                                pe.wait_ge(drained[X_BANKS[k % 4]], X_USES[k % 4] + k // 4)
                            piece(k, (2 * (k - at), 2 * (k - at) + 1), hT_hi, hT_lo, b, k == at, k == at + 7)
                if k + 2 < KD // 2:
                    x_turned(k + 2)
                if k == 7:
                    pe.wait_ge(p_in, 16)
                    turned(BT, T_PLE, [p_nat[:, t, q * P:(q + 1) * P] for q in range(2) for t in range(TT)])
                if k == 8:
                    pe.wait_ge(vec_in, 144)
                    turned(BT, T_VEC, [vecs[:, :]])
                if k == P_A2 + 1:
                    pe.wait_ge(acc_out[1], 1)
                    turned(BT, T_SMALL, [th[0:N_SMALL, 0, TH_SMALL + t * P:TH_SMALL + (t + 1) * P] for t in range(TT)])
                if k == P_A2 + 3:
                    pe.wait_ge(drained[BT], T_SMALL)
                    turned(BT, T_IK, [th[:, t, TH_IK2:TH_IK2 + P] for t in range(TT)])
                for u, at in enumerate((14, 15, 19, 20)):
                    if k == at:
                        pe.wait_ge(acc_out[0], 1 + u // 2)
                        turned(BT, T_IQ + u, [th[:, t, (2 * u + q) * P:(2 * u + q + 1) * P] for q in range(2) for t in range(TT)])
                for hh in range(0, IH, 2):
                    if k == (16 + hh // 2 if hh < 8 else 18 + hh // 2):
                        pe.wait_ge(drained[BT], T_IQ + (1 if hh < 8 else 3))
                        index_head(hh)
                        index_head(hh + 1)
                for kv in range(2):
                    if k == 27 + kv:
                        pe.wait_ge(acc_out[1], 2)
                        col = TH_KC + kv * 256
                        turned(BT, T_KC + kv, [th[:, t, col + grp * DH:col + (grp + 1) * DH]
                                               for grp in range(GROUPS) for t in range(TT)])
                for br, at, n, col in ((0, 46, T_KS, TH_KS), (1, 53, T_KW, TH_KW), (2, 69, T_DK, TH_DK)):
                    if k == at:
                        pe.wait_ge(kn_ready, 4 * (br + 1))
                        turned(BT, n, [th[:, t, col + grp * DH:col + (grp + 1) * DH] for grp in range(GROUPS) for t in range(TT)])
                for kv in range(2):
                    if k == 49 + 16 * kv:
                        pe.wait_ge(hid_out, kv + 1)
                        rows = th[0:2 * NB, 1, TH_HID:TH_HID + HID]
                        o = aux[BS0 + kv][0:NB, HID:2 * HID]
                        m.matmul(o, ident[0:2 * NB, 0:NB], rows, start=True, stop=False)
                        m.matmul(o, ident[0:2 * NB, NB:2 * NB], rows, start=False, stop=True).then_inc(filled[BS0 + kv], 1)
                    if k == 52 + 16 * kv:
                        pe.wait_ge(hid_ready, kv + 1)
                        turned(BT, (T_HK, T_HV)[kv], [hth[:, kv, q * P:(q + 1) * P] for q in range(2)])
                if k == 54:
                    bank_free(BT, T_KC2)
                    pe.wait_ge(w2_in, 32)
                    for q in range(2):
                        e = m.matmul(aux[BT][0:NB, 0:DH], hidT[:, q, :], w2[:, 0, q, :], start=(q == 0), stop=(q == 1))
                    e.then_inc(filled[BT], 1)
                if k == 70:
                    bank_free(BT, T_VC2)
                    for grp in range(GROUPS):
                        for q in range(2):
                            e = m.matmul(aux[BT][0:NC, DH * grp:DH * (1 + grp)], hidT[:, 2 + q, grp * NC:(grp + 1) * NC],
                                         w2[:, 1, q, :], start=(q == 0), stop=(q == 1))
                    e.then_inc(filled[BT], 1)
                if k == 58:
                    pe.wait_ge(kcn_ready, 1)
                    turned(BT, T_KCN, [kc_nat[:, :]])

            def dots(b, mix, br, g):
                keys = kT[:, br, bass.ds(g, 1), :].rearrange("p g t -> p (g t)")
                for t in range(TT):
                    e = m.matmul(aux[b][:, t * P:(2 * t + 1) * P], qT[:, mix, t * P:(t + 1) * P],
                                 keys[:, 0:(t + 1) * P], start=True, stop=True)
                return e

            def probs_turned(n, br):
                bank_free(BT, n)
                for q in range(3):
                    e = m.transpose(aux[BT][:, q * P:(q + 1) * P], prob[:, br, q * P:(q + 1) * P], ident[:, :])
                e.then_inc(filled[BT], 1)

            def weighted(b, at, br, g):
                vals = [v_all[:, br, kt, bass.ds(g, 1), :].rearrange("p g d -> p (g d)") for kt in range(TT)]
                m.matmul(aux[b][:, at:at + P], probT[:, br, 0:P], vals[0], start=True, stop=True)
                m.matmul(aux[b][:, at + P:at + 2 * P], probT[:, br, P:2 * P], vals[0], start=True, stop=False)
                return m.matmul(aux[b][:, at + P:at + 2 * P], probT[:, br, 2 * P:3 * P], vals[1], start=False, stop=True)

            def attend(k, i):
                g = i // 4
                nT = i * 5 + T_L
                if k == 2:
                    pe.wait_ge(qn_ready, i + 1)
                    bank_free(BT, nT)
                    for mix in range(2):
                        for t in range(TT):
                            e = m.transpose(aux[BT][:, mix * T + t * P:mix * T + (t + 1) * P], q_n[:, t, mix, :], ident[:, :])
                    e.then_inc(filled[BT], 1)
                if k == 3:
                    pe.wait_ge(drained[BT], nT)
                    bank_free(BS0, i * 2 + S_L)
                    dots(BS0, 0, 0, g)
                    ck = kcT[:, bass.ds(g * NC, NC)]
                    for t in range(TT):
                        e = m.matmul(aux[BS0][:, 3 * P + t * 16:3 * P + t * 16 + NC], qT[:, 0, t * P:(t + 1) * P], ck,
                                     start=True, stop=True)
                    e.then_inc(filled[BS0], 1)
                    bank_free(BS1, i * 2 + S_L)
                    dots(BS1, 0, 1, g).then_inc(filled[BS1], 1)
                if k == 4:
                    bank_free(BS0, i * 2 + S_L + 1)
                    dots(BS0, 1, 2, g).then_inc(filled[BS0], 1)
                if k == 5:
                    pe.wait_ge(exp_ready, i * 3 + 1)
                    probs_turned(nT + 1, 0)
                    bank_free(BO, i * 2 + O_L)
                    for t in range(TT):
                        e = m.transpose(aux[BO][0:NC, t * P:(t + 1) * P], prob_c[:, t, :], ident[:, :])
                    e.then_inc(filled[BO], 1)
                if k == 6:
                    pe.wait_ge(exp_ready, i * 3 + 2)
                    probs_turned(nT + 2, 1)
                    bank_free(BO, i * 2 + O_L + 1)
                    cv = vc[:, bass.ds(g, 1), :].rearrange("p g d -> p (g d)")
                    for t in range(TT):
                        m.matmul(aux[BO][:, t * P:(t + 1) * P], prob_cT[:, t * P:(t + 1) * P], cv, start=True, stop=True)
                    weighted(BO, T, 0, g).then_inc(filled[BO], 1)
                if k == 7:
                    pe.wait_ge(exp_ready, i * 3 + 3)
                    probs_turned(nT + 3, 2)
                    bank_free(BS1, i * 2 + S_L + 1)
                    weighted(BS1, 0, 1, g)
                if k == 8:
                    pe.wait_ge(drained[BT], nT + 3)
                    weighted(BS1, T, 2, g).then_inc(filled[BS1], 1)
                if k == 10:
                    pe.wait_ge(o_ready, i + 1)
                    bank_free(BT, nT + 4)
                    for mix in range(2):
                        for t in range(TT):
                            e = m.transpose(aux[BT][:, mix * T + t * P:mix * T + (t + 1) * P], o_nat[:, mix, t, :], ident[:, :])
                    e.then_inc(filled[BT], 1)

            with pe.Fori(0, HEADS - 1) as i:
                for k in range(8):
                    if k == 0:
                        pe.wait_ge(acc_out[0], i + ACC_L)
                    piece(P_L + k, (2 * k, 2 * k + 1), hT_hi, hT_lo, 0, k == 0, k == 7, i=i, per=16)
                    attend(k, i)
                pe.wait_ge(acc_out[1], i + ACC_L)
                for k in range(8):
                    piece(P_L + 8 + k, (2 * k, 2 * k + 1), hT_hi, hT_lo, 1, k == 0, k == 7, i=i, per=16)
                    attend(8 + k, i)
            pe.wait_ge(acc_out[0], ACC_L + HEADS - 1)
            for k in range(8):
                piece(P_L7 + k, (2 * k, 2 * k + 1), hT_hi, hT_lo, 0, k == 0, k == 7)
                attend(k, HEADS - 1)

            def y_turned(j):
                pe.wait_ge(y_ready, j + 1)
                for b, n, o in ((BT, T_Y, 0), (BO, O_Y, 2)):
                    bank_free(b, j + n)
                    for q in range(2):
                        for t in range(TT):
                            e = m.transpose(aux[b][:, q * T + t * P:q * T + (t + 1) * P],
                                            stage[:, t, (o + q) * P:(o + q + 1) * P], ident[:, :])
                    e.then_inc(filled[b], 1)

            def up_block(j, first):
                for k in range(8):
                    b, half = 1 - k // 2 % 2, k // 4
                    if k == 0:
                        pe.wait_ge(acc_out[1], j + ACC_L + 7)
                    if k == 2:
                        pe.wait_ge(acc_out[0], j + ACC_L + 8)
                    if k == 4 and first:
                        pe.wait_ge(drained[BT], T_Y - 1)
                    kt = (1 - b) * HEADS + 4 * half + 2 * (k % 2)
                    piece(P_U + k, (kt, kt + 1), oT_hi, oT_lo, b, k in (0, 2), k in (5, 7), i=j, per=8)
                    if k == 1 and not first:
                        y_turned(j - 1)
                    if first:
                        attend(8 + k, HEADS - 1)

            up_block(0, True)
            with pe.Fori(1, 4) as j:
                up_block(j, False)
            for k in range(4):
                pe.wait_ge(acc_out[1 - k % 2], ACC_L + (11, 12)[k % 2] + k // 2)
                for kt in range(2):
                    e = piece(P_PP + k // 2 * 2 + kt, (kt,), pT_hi, pT_lo, 1 - k % 2, kt == 0, kt == 1, at=k % 2 * NCOL)
                    if k % 2:
                        e.then_inc(piece_used, 1)
                    elif kt:
                        e.then_inc(ple_made, 1)
                if k == 1:
                    y_turned(3)

            def x2_turned(j):
                pe.wait_ge(acc_out[(j + 1) % 2], ACC_L + (14, 15, 15, 16)[j])
                for b, n, o in ((BT, T_X, 0), (BO, O_X, 2)):
                    bank_free(b, j + n)
                    for q in range(2):
                        for t in range(TT):
                            c = j * NCOL + (o + q) * P
                            e = m.transpose(aux[b][:, q * T + t * P:q * T + (t + 1) * P], xr[:, t, c:c + P], ident[:, :])
                    e.then_inc(filled[b], 1)

            for j in range(4):
                b, n = (j + 1) % 2, ACC_L + (13, 14, 14, 15)[j]
                pe.wait_ge(acc_out[b], n)
                for k in range(8):
                    if j == 0:
                        pe.wait_ge(drained[(BT, BO)[k % 2]], (T_Y, O_Y)[k % 2] + k // 2)
                    piece(P_O + 8 * j + k, (2 * k, 2 * k + 1), hT_hi, hT_lo, b, k == 0, k == 7)
                    if j and k == 2:
                        x2_turned(j - 1)
            for j in range(4):
                b = (j + 1) % 2
                if j < 2:
                    pe.wait_ge(acc_out[b], ACC_L + 15 + j)
                else:
                    pe.wait_ge(g_tanh, 2 * j - 2)
                for k in range(8 if j < 3 else 6):
                    if j == 0:
                        pe.wait_ge(drained[(BT, BO)[k % 2]], (T_X, O_X)[k % 2] + k // 2)
                    piece(P_G + 8 * j + k, (2 * k, 2 * k + 1), oT_hi, oT_lo, b, k == 0, k == 7)
                    if j == 0 and k == 2:
                        x2_turned(3)
            for t in range(TT):
                for k in (6, 7):
                    e = piece(N_PIECES - 8 + k, (2 * k, 2 * k + 1), oT_hi, oT_lo, 0, False, k == 7, tiles=(t,), at=0)
                    if t:
                        e.then_inc(piece_used, 1)
                    elif k == 7:
                        e.then_inc(first_tile_done, 1)


_INS = ["x", "p", "norm_g", "w_in", "nsa_q_g", "nsa_kc_g", "nsa_ks_g", "nsa_kw_g", "cmp_pe_k", "cmp_w1_k", "cmp_w2_k",
        "cmp_pe_v", "cmp_w1_v", "cmp_w2_v", "dsa_q_g", "dsa_k_g", "w_up_nsa", "w_up_dsa", "w_out", "ple_norm_g",
        "w_ple_gate", "w_ple_proj"]
_OUTS = [((1, T, D), "float32")]


def kernel(**inputs):
    import numpy as _np
    import concourse.bacc as _bacc
    from concourse import mybir as _mybir
    from concourse.bass_utils import run_bass_kernel_spmd as _run

    nc = _bacc.Bacc("TRN2", target_bir_lowering=False, num_devices=1)
    arrays, args = {}, []
    for name in _INS:
        a = _np.ascontiguousarray(inputs[name])
        arrays[f"in_{name}_dram"] = a
        args.append(nc.dram_tensor(f"in_{name}_dram", a.shape, _mybir.dt.from_np(a.dtype), kind="ExternalInput").ap())
    for i, (shape, dtype) in enumerate(_OUTS):
        dt = _mybir.dt.from_np(_np.dtype(dtype))
        args.append(nc.dram_tensor(f"out_{i}_dram", shape, dt, kind="ExternalOutput").ap())
    build(nc, *args)
    r = _run(nc, [arrays], core_ids=[0])
    got = tuple(r.results[0][f"out_{i}_dram"] for i in range(len(_OUTS)))
    return got[0]
```
